# Optimizing a Trainium2 kernel written in Bass

```python
import jax, jax.numpy as jnp
from jax import lax
import numpy as np

D_MODEL = 1024
BATCH = 1
SEQ = 512
DEPTH = 1

D_PLE = 256
HEAD_DIM = 64
ROPE_DIM = HEAD_DIM // 4
ROPE_THETA = 500000.0
N_HEADS_A = 8
N_HEADS_B = 8
WIDTH_A = N_HEADS_A * HEAD_DIM
WIDTH_B = N_HEADS_B * HEAD_DIM
N_IDX_HEADS = 8
IDX_DIM = 64
TOPK_MAX = 256
Q_BLOCK = 128
EPS = 1e-6
NEG = -1e30

SPLITS = (WIDTH_A, HEAD_DIM, HEAD_DIM, WIDTH_A,
          N_IDX_HEADS * IDX_DIM, IDX_DIM, N_IDX_HEADS,
          WIDTH_B, WIDTH_B, WIDTH_B, N_HEADS_B, WIDTH_B)
D_IN = sum(SPLITS)


def _offsets():
    offs, acc = [], 0
    for w in SPLITS[:-1]:
        acc += w
        offs.append(acc)
    return offs

def rmsnorm(x, g):
    xf = x.astype(jnp.float32)
    y = xf * lax.rsqrt(jnp.mean(xf * xf, axis=-1, keepdims=True) + EPS) * g.astype(jnp.float32)
    return y.astype(x.dtype)

def partial_rope(x, pos):
    half = ROPE_DIM // 2
    freqs = ROPE_THETA ** (-jnp.arange(half, dtype=jnp.float32) / half)
    ang = pos.astype(jnp.float32)[:, None] * freqs[None, :]
    cos = jnp.cos(ang)[None, :, None, :]
    sin = jnp.sin(ang)[None, :, None, :]
    x1 = x[..., :half].astype(jnp.float32)
    x2 = x[..., half:ROPE_DIM].astype(jnp.float32)
    rot = jnp.concatenate([x1 * cos - x2 * sin, x2 * cos + x1 * sin], axis=-1).astype(x.dtype)
    return jnp.concatenate([rot, x[..., ROPE_DIM:]], axis=-1)

def to_blocks(t):
    B, S = t.shape[:2]
    t = t.reshape((B, S // Q_BLOCK, Q_BLOCK) + t.shape[2:])
    return jnp.moveaxis(t, 1, 0)

def from_blocks(t):
    t = jnp.moveaxis(t, 0, 1)
    return t.reshape((t.shape[0], t.shape[1] * t.shape[2]) + t.shape[3:])

def dsa_branch(qa, ka, va, qi, ki, wi):
    B, S = ka.shape[:2]
    topk = min(TOPK_MAX, S // 4)
    nb = S // Q_BLOCK
    key_pos = jnp.arange(S)
    scale = HEAD_DIM ** -0.5

    def block(args):
        blk, q_blk, qi_blk, wi_blk = args
        q_pos = blk * Q_BLOCK + jnp.arange(Q_BLOCK)
        causal = key_pos[None, :] <= q_pos[:, None]
        dots = jnp.einsum('bqhd,bsd->bqhs', qi_blk, ki)
        score = jnp.einsum('bqhs,bqh->bqs', jax.nn.relu(dots).astype(jnp.float32),
                           wi_blk.astype(jnp.float32))
        score = jnp.where(causal[None], score, -jnp.inf)
        _, sel = lax.top_k(score, topk)
        k_sel = jax.vmap(lambda k, i: k[i])(ka, sel)
        v_sel = jax.vmap(lambda v, i: v[i])(va, sel)
        logits = jnp.einsum('bqhd,bqkd->bhqk', q_blk, k_sel).astype(jnp.float32) * scale
        valid = sel <= q_pos[None, :, None]
        logits = jnp.where(valid[:, None], logits, NEG)
        probs = jax.nn.softmax(logits, axis=-1).astype(v_sel.dtype)
        return jnp.einsum('bhqk,bqkd->bqhd', probs, v_sel)

    out = lax.map(block, (jnp.arange(nb), to_blocks(qa), to_blocks(qi), to_blocks(wi)))
    return from_blocks(out)

def fox_branch(qb, kb, vb, log_f):
    B, S = qb.shape[:2]
    nb = S // Q_BLOCK
    key_pos = jnp.arange(S)
    scale = HEAD_DIM ** -0.5
    c = jnp.cumsum(log_f, axis=1)
    c_k = jnp.transpose(c, (0, 2, 1))

    def block(args):
        blk, q_blk, cq_blk = args
        q_pos = blk * Q_BLOCK + jnp.arange(Q_BLOCK)
        causal = key_pos[None, :] <= q_pos[:, None]
        logits = jnp.einsum('bqhd,bshd->bhqs', q_blk, kb).astype(jnp.float32) * scale
        logits = logits + jnp.transpose(cq_blk, (0, 2, 1))[..., None] - c_k[:, :, None, :]
        logits = jnp.where(causal[None, None], logits, NEG)
        probs = jax.nn.softmax(logits, axis=-1).astype(vb.dtype)
        return jnp.einsum('bhqs,bshd->bqhd', probs, vb)

    out = lax.map(block, (jnp.arange(nb), to_blocks(qb), to_blocks(c)))
    return from_blocks(out)

def first_inputs(seed: int = 0) -> dict:
    key = jax.random.key(seed)
    ks = jax.random.split(key, 14)
    f32 = jnp.float32
    nrm = lambda k, shape, fan_in: jax.random.normal(k, shape, f32) * (fan_in ** -0.5)
    x = jax.random.normal(ks[0], (BATCH, SEQ, D_MODEL), f32)
    p = jax.random.normal(ks[1], (DEPTH, BATCH, SEQ, D_PLE), f32)
    w_in = nrm(ks[2], (DEPTH, D_MODEL, D_IN), D_MODEL)
    b_forget = jax.random.uniform(ks[3], (DEPTH, N_HEADS_B), f32, 1.0, 5.0)
    w_branch_a = nrm(ks[4], (DEPTH, WIDTH_A, D_MODEL), WIDTH_A)
    w_branch_b = nrm(ks[5], (DEPTH, WIDTH_B, D_MODEL), WIDTH_B)
    w_merge = nrm(ks[6], (DEPTH, D_MODEL, 2 * D_MODEL), D_MODEL)
    w_out = nrm(ks[7], (DEPTH, D_MODEL, D_MODEL), D_MODEL)
    g_pre = 1.0 + 0.02 * jax.random.normal(ks[8], (DEPTH, D_MODEL), f32)
    g_post = 1.0 + 0.02 * jax.random.normal(ks[9], (DEPTH, D_MODEL), f32)
    w_ple = nrm(ks[10], (DEPTH, D_PLE, D_MODEL), D_PLE)
    w_ple_gate = nrm(ks[11], (DEPTH, D_MODEL, D_MODEL), D_MODEL)
    g_ple = 1.0 + 0.02 * jax.random.normal(ks[12], (DEPTH, D_MODEL), f32)
    return {"x": x, "p": p, "w_in": w_in, "b_forget": b_forget,
            "w_branch_a": w_branch_a, "w_branch_b": w_branch_b, "w_merge": w_merge,
            "w_out": w_out, "g_pre": g_pre, "g_post": g_post, "w_ple": w_ple,
            "w_ple_gate": w_ple_gate, "g_ple": g_ple}

def first_block(x, p, w_in, b_forget, w_branch_a, w_branch_b, w_merge, w_out,
              g_pre, g_post, w_ple, w_ple_gate, g_ple):
    B, S, _ = x.shape
    pos = jnp.arange(S)
    offs = _offsets()
    idx_scale = (N_IDX_HEADS ** -0.5) * (IDX_DIM ** -0.5)
    for i in range(DEPTH):
        h = rmsnorm(x, g_pre[i])
        proj = h @ w_in[i]
        (qa, ka, va, gate_a, qi, ki, wi, qb, kb, vb, fb, gate_b) = jnp.split(proj, offs, axis=-1)

        qa = partial_rope(qa.reshape(B, S, N_HEADS_A, HEAD_DIM), pos)
        ka = partial_rope(ka.reshape(B, S, 1, HEAD_DIM), pos).reshape(B, S, HEAD_DIM)
        qi = partial_rope(qi.reshape(B, S, N_IDX_HEADS, IDX_DIM), pos)
        ki = partial_rope(ki.reshape(B, S, 1, IDX_DIM), pos).reshape(B, S, IDX_DIM)
        wi = wi * idx_scale
        att_a = dsa_branch(qa, ka, va, qi, ki, wi).reshape(B, S, WIDTH_A)
        y_a = (att_a * jax.nn.silu(gate_a)) @ w_branch_a[i]

        log_f = jax.nn.log_sigmoid(fb.astype(jnp.float32) + b_forget[i].astype(jnp.float32))
        att_b = fox_branch(qb.reshape(B, S, N_HEADS_B, HEAD_DIM),
                           kb.reshape(B, S, N_HEADS_B, HEAD_DIM),
                           vb.reshape(B, S, N_HEADS_B, HEAD_DIM), log_f).reshape(B, S, WIDTH_B)
        y_b = (att_b * jax.nn.silu(gate_b)) @ w_branch_b[i]

        m_a, m_b = jnp.split(jax.nn.sigmoid(h @ w_merge[i]), 2, axis=-1)
        out = (m_a * y_a + m_b * y_b) @ w_out[i]
        x = x + rmsnorm(out, g_post[i])

        e = p[i] @ w_ple[i]
        gate = jax.nn.sigmoid(x @ w_ple_gate[i])
        x = x + rmsnorm(gate * e, g_ple[i])
    return x


ROPE_THETA_2 = 10000.0
BLOCK = 128

SWA_HEADS = 8
SWA_KV_HEADS = 2
SWA_GROUP = SWA_HEADS // SWA_KV_HEADS
WINDOW = 128

MLA_HEADS = 8
MLA_NOPE_DIM = 64
MLA_ROPE_DIM = 32
MLA_V_DIM = 64
MLA_QK_DIM = MLA_NOPE_DIM + MLA_ROPE_DIM
Q_LORA_RANK = 384
KV_LORA_RANK = 256

D_FF = -(-8 * D_MODEL // (3 * 256)) * 256

IN_SIZES = [
    SWA_HEADS * HEAD_DIM,
    SWA_KV_HEADS * HEAD_DIM,
    SWA_KV_HEADS * HEAD_DIM,
    Q_LORA_RANK,
    KV_LORA_RANK,
    MLA_ROPE_DIM,
    D_MODEL,
    D_MODEL,
]
IN_WIDTH = int(sum(IN_SIZES))
IN_OFFSETS = [int(v) for v in np.cumsum(IN_SIZES)[:-1]]


def rmsnorm_2(x, g):
    xf = x.astype(jnp.float32)
    xf = xf * lax.rsqrt(jnp.mean(xf * xf, axis=-1, keepdims=True) + EPS)
    return (xf * g.astype(jnp.float32)).astype(x.dtype)

def rope_tables(seq, dim):
    inv = ROPE_THETA_2 ** (-jnp.arange(0, dim, 2, dtype=jnp.float32) / dim)
    ang = jnp.arange(seq, dtype=jnp.float32)[:, None] * inv[None, :]
    return jnp.cos(ang)[:, None, :], jnp.sin(ang)[:, None, :]

def apply_rope(x, cos, sin):
    xf = x.astype(jnp.float32)
    x1, x2 = jnp.split(xf, 2, axis=-1)
    out = jnp.concatenate([x1 * cos - x2 * sin, x2 * cos + x1 * sin], axis=-1)
    return out.astype(x.dtype)

def swa_sink_attention(q, k, v, sinks):
    B, S = q.shape[0], q.shape[1]
    nb = S // BLOCK
    qb = q.reshape(B, nb, BLOCK, SWA_KV_HEADS, SWA_GROUP, HEAD_DIM)

    def band(t):
        tp = jnp.pad(t, ((0, 0), (BLOCK, 0), (0, 0), (0, 0)))
        tb = tp.reshape(B, nb + 1, BLOCK, SWA_KV_HEADS, HEAD_DIM)
        return jnp.concatenate([tb[:, :-1], tb[:, 1:]], axis=2)

    kw, vw = band(k), band(v)
    s = jnp.einsum('bnqhgd,bnkhd->bnhgqk', qb, kw,
                   preferred_element_type=jnp.float32) * (HEAD_DIM ** -0.5)
    qi = jnp.arange(BLOCK)[:, None]
    kj = jnp.arange(2 * BLOCK)[None, :]
    diff = qi - kj + BLOCK
    band_ok = (diff >= 0) & (diff < WINDOW)
    kpos = jnp.arange(nb)[:, None] * BLOCK + kj - BLOCK
    mask = band_ok[None] & (kpos >= 0)[:, None, :]
    s = jnp.where(mask[None, :, None, None], s, -jnp.inf)
    sink = sinks.astype(jnp.float32).reshape(1, 1, SWA_KV_HEADS, SWA_GROUP, 1, 1)
    m = jnp.maximum(jnp.max(s, axis=-1, keepdims=True), sink)
    p = jnp.exp(s - m)
    denom = jnp.sum(p, axis=-1, keepdims=True) + jnp.exp(sink - m)
    p = (p / denom).astype(v.dtype)
    o = jnp.einsum('bnhgqk,bnkhd->bnqhgd', p, vw)
    return o.reshape(B, S, SWA_HEADS * HEAD_DIM)

def mla_attention(q_nope, q_rope, k_nope, k_rope, v):
    B, S = q_nope.shape[0], q_nope.shape[1]
    nb = S // BLOCK
    scale = MLA_QK_DIM ** -0.5
    kpos = jnp.arange(S)

    def to_blocks(t):
        return jnp.moveaxis(t.reshape(B, nb, BLOCK, *t.shape[2:]), 1, 0)

    def one_block(args):
        qn, qr, n = args
        s = (jnp.einsum('bqhd,bkhd->bhqk', qn, k_nope, preferred_element_type=jnp.float32)
             + jnp.einsum('bqhr,bkr->bhqk', qr, k_rope, preferred_element_type=jnp.float32)) * scale
        qpos = n * BLOCK + jnp.arange(BLOCK)
        causal = kpos[None, :] <= qpos[:, None]
        s = jnp.where(causal[None, None], s, -jnp.inf)
        p = jax.nn.softmax(s, axis=-1).astype(v.dtype)
        return jnp.einsum('bhqk,bkhd->bqhd', p, v)

    o = lax.map(one_block, (to_blocks(q_nope), to_blocks(q_rope), jnp.arange(nb)))
    return jnp.moveaxis(o, 0, 1).reshape(B, S, MLA_HEADS * MLA_V_DIM)

def second_inputs(seed: int = 0) -> dict:
    key = jax.random.key(seed)
    ks = jax.random.split(key, 17)
    f32 = jnp.float32

    def w(k, shape, fan_in):
        return jax.random.normal(k, shape, f32) * (fan_in ** -0.5)

    def gain(k, shape):
        return 1.0 + 0.02 * jax.random.normal(k, shape, f32)

    L = DEPTH
    return {
        "x": jax.random.normal(ks[0], (BATCH, SEQ, D_MODEL), f32),
        "mix_norm_g": gain(ks[1], (L, D_MODEL)),
        "w_in": w(ks[2], (L, D_MODEL, IN_WIDTH), D_MODEL),
        "swa_sinks": 0.5 * jax.random.normal(ks[3], (L, SWA_HEADS), f32),
        "q_norm_g": gain(ks[4], (L, Q_LORA_RANK)),
        "w_uq": w(ks[5], (L, Q_LORA_RANK, MLA_HEADS * MLA_QK_DIM), Q_LORA_RANK),
        "kv_norm_g": gain(ks[6], (L, KV_LORA_RANK)),
        "w_ukv": w(ks[7], (L, KV_LORA_RANK, MLA_HEADS * (MLA_NOPE_DIM + MLA_V_DIM)), KV_LORA_RANK),
        "w_o_swa": w(ks[8], (L, SWA_HEADS * HEAD_DIM, D_MODEL), SWA_HEADS * HEAD_DIM),
        "w_o_mla": w(ks[9], (L, MLA_HEADS * MLA_V_DIM, D_MODEL), MLA_HEADS * MLA_V_DIM),
        "w_out": w(ks[10], (L, D_MODEL, D_MODEL), D_MODEL),
        "ffn_norm_g": gain(ks[11], (L, D_MODEL)),
        "w_gate": w(ks[12], (L, D_MODEL, D_FF), D_MODEL),
        "w_up": w(ks[13], (L, D_MODEL, D_FF), D_MODEL),
        "w_down": w(ks[14], (L, D_FF, D_MODEL), D_FF),
        "final_norm_g": gain(ks[15], (D_MODEL,)),
    }

def second_block(x, mix_norm_g, w_in, swa_sinks, q_norm_g, w_uq, kv_norm_g, w_ukv,
              w_o_swa, w_o_mla, w_out, ffn_norm_g, w_gate, w_up, w_down, final_norm_g):
    B, S = x.shape[0], x.shape[1]
    cos_a, sin_a = rope_tables(S, HEAD_DIM)
    cos_b, sin_b = rope_tables(S, MLA_ROPE_DIM)

    for l in range(DEPTH):
        h = rmsnorm_2(x, mix_norm_g[l])
        proj = h @ w_in[l]
        qa, ka, va, q_lat, kv_lat, k_r, g_a, g_b = jnp.split(proj, IN_OFFSETS, axis=-1)

        qa = apply_rope(qa.reshape(B, S, SWA_HEADS, HEAD_DIM), cos_a, sin_a)
        ka = apply_rope(ka.reshape(B, S, SWA_KV_HEADS, HEAD_DIM), cos_a, sin_a)
        va = va.reshape(B, S, SWA_KV_HEADS, HEAD_DIM)
        o_a = swa_sink_attention(qa, ka, va, swa_sinks[l])

        cq = rmsnorm_2(q_lat, q_norm_g[l])
        qb = (cq @ w_uq[l]).reshape(B, S, MLA_HEADS, MLA_QK_DIM)
        q_nope, q_rope = jnp.split(qb, [MLA_NOPE_DIM], axis=-1)
        q_rope = apply_rope(q_rope, cos_b, sin_b)
        ckv = rmsnorm_2(kv_lat, kv_norm_g[l])
        kvb = (ckv @ w_ukv[l]).reshape(B, S, MLA_HEADS, MLA_NOPE_DIM + MLA_V_DIM)
        k_nope, vb = jnp.split(kvb, [MLA_NOPE_DIM], axis=-1)
        k_rope = apply_rope(k_r[:, :, None, :], cos_b, sin_b)[:, :, 0, :]
        o_b = mla_attention(q_nope, q_rope, k_nope, k_rope, vb)

        y = jax.nn.sigmoid(g_a) * (o_a @ w_o_swa[l]) + jax.nn.sigmoid(g_b) * (o_b @ w_o_mla[l])
        x = x + y @ w_out[l]

        h = rmsnorm_2(x, ffn_norm_g[l])
        x = x + (jax.nn.silu(h @ w_gate[l]) * (h @ w_up[l])) @ w_down[l]

    return rmsnorm_2(x, final_norm_g)


def setup_inputs(seed=0):
    out = dict(first_inputs(seed))
    for name, value in second_inputs(seed + 1).items():
        if name != "x":
            out[name + "_2"] = value
    return out


def reference(
    x, p, w_in, b_forget, w_branch_a, w_branch_b, w_merge, w_out, g_pre, g_post, w_ple,
    w_ple_gate, g_ple, mix_norm_g_2, w_in_2, swa_sinks_2, q_norm_g_2, w_uq_2, kv_norm_g_2,
    w_ukv_2, w_o_swa_2, w_o_mla_2, w_out_2, ffn_norm_g_2, w_gate_2, w_up_2, w_down_2,
    final_norm_g_2,
):
    x = first_block(
        x, p, w_in, b_forget, w_branch_a, w_branch_b, w_merge, w_out, g_pre, g_post, w_ple,
        w_ple_gate, g_ple,
    )
    return second_block(
        x, mix_norm_g_2, w_in_2, swa_sinks_2, q_norm_g_2, w_uq_2, kv_norm_g_2, w_ukv_2,
        w_o_swa_2, w_o_mla_2, w_out_2, ffn_norm_g_2, w_gate_2, w_up_2, w_down_2, final_norm_g_2,
    )


_drawn_inputs = setup_inputs


def setup_inputs(seed=0):
    import zlib

    import numpy as np

    out = dict(_drawn_inputs(seed))
    spreads = {}
    factors = {'g_post': 4.427,
     'g_ple': 4.707,
     'mix_norm_g_2': 8.0,
     'swa_sinks_2': 182.463,
     'q_norm_g_2': 8.0,
     'kv_norm_g_2': 8.0,
     'ffn_norm_g_2': 5.708,
     'final_norm_g_2': 23.931}
    for name, (base, spread) in spreads.items():
        noise = np.random.default_rng([zlib.crc32(name.encode()), seed]).standard_normal(out[name].shape)
        drawn = base * np.exp(spread * noise) if base else spread * noise
        out[name] = __import__('jax').numpy.asarray(drawn.astype(out[name].dtype))
    for name, factor in factors.items():
        out[name] = (out[name] * factor).astype(out[name].dtype)
    return out
```

```python
from contextlib import ExitStack

import numpy as np

import concourse.bass as bass
from concourse import mybir

F32 = mybir.dt.float32
F32R = mybir.dt.float32r
BF16 = mybir.dt.bfloat16
ALU = mybir.AluOpType
ACT = mybir.ActivationFunctionType

P = 128
S = 512
NB = S // P
D = 1024
KD = D // P
DH = 64
H = 8
WA = H * DH
TOPK = min(256, S // 4)
EPS = 1e-6
NEG = -1e30
TAKEN = -3e38
D_PLE = 256
QR, KVR, MR = 384, 256, 32
MQK = DH + MR
DFF = 2816
CH = 2048

O_QA, O_KA, O_GA, O_QI, O_KI = 0, 512, 640, 1152, 1664
O_QB, O_KB, O_VB, O_FB, O_GB = 1736, 2248, 2760, 3272, 3280
O2_Q, O2_KV, O2_QL, O2_KVL, O2_GA, O2_GB = 0, 512, 768, 1152, 1440, 2464
SM_W = 208
SM_KI, SM_WI, SM_FB, SM_KA, SM_VA = 0, 64, 72, 80, 144

_C = {}
_at = 0
for _n, _w in (("ident", P), ("causal", 3 * P + P), ("cum", 3 * P + S), ("band", 2 * P),
               ("cos1", NB * 8), ("sin1", NB * 8), ("cos2", NB * 32), ("sin2", NB * 32),
               ("cos3", NB * 16), ("sin3", NB * 16)):
    _C[_n] = (_at, _w)
    _at += _w
CST_W = _at
GV = {"pre": 0, "post": 8, "ple": 16, "mix": 24, "ffn": 32, "q": 40, "kv": 43}
GV_W = 45


def constants():
    f = np.float32
    c = np.zeros((P, CST_W), f)
    q = np.arange(P)[:, None]

    def put(name, a):
        o, w = _C[name]
        c[:, o:o + w] = a

    put("ident", np.eye(P, dtype=f))
    k = np.arange(4 * P)[None, :] - 3 * P
    put("causal", np.where(k <= q, 0, NEG).astype(f))
    k = np.arange(3 * P + S)[None, :] - 3 * P
    put("cum", np.where(k >= q, 1, 0).astype(f))
    kj = np.arange(2 * P)[None, :]
    diff = q - kj + P
    put("band", np.where((diff >= 0) & (diff < P), 0, NEG).astype(f))
    pos = (np.arange(NB)[None, :, None] * P + np.arange(P)[:, None, None]).astype(f)
    for n, half, freqs in (
        ("1", 8, f(500000.0) ** (-np.arange(8, dtype=f) / f(8))),
        ("2", 32, f(10000.0) ** (-np.arange(0, 64, 2, dtype=f) / f(64))),
        ("3", 16, f(10000.0) ** (-np.arange(0, 32, 2, dtype=f) / f(32))),
    ):
        ang = (pos * freqs.astype(f)[None, None, :]).astype(f)
        put("cos" + n, np.cos(ang).reshape(P, NB * half))
        put("sin" + n, np.sin(ang).reshape(P, NB * half))
    return c


def plan_weights():
    chunks, units = [], {}

    def unit(name, rows, per, pieces):
        first, n = len(chunks), sum(w for _, _, w in pieces)
        for k in range(0, rows // P, per):
            off, ps = 0, []
            for arr, col, w in pieces:
                ps.append((arr, k * P, col, w, off))
                off += w
            assert per * n <= CH
            chunks.append((per, n, ps))
        units[name] = (first, rows // P // per, per, n)

    w1, w2 = "w_in", "w_in_2"
    unit("qi", D, 4, [(w1, O_QI, WA)])
    unit("sm", D, 8, [(w1, O_KI, 72), (w1, O_FB, 8), (w1, O_KA, 128)])
    unit("qa", D, 4, [(w1, O_QA, WA)])
    unit("qb", D, 4, [(w1, O_QB, WA)])
    unit("kb", D, 4, [(w1, O_KB, WA)])
    unit("vb", D, 4, [(w1, O_VB, WA)])
    unit("ga", D, 4, [(w1, O_GA, WA)])
    unit("gb", D, 4, [(w1, O_GB, WA)])
    for n, arr in (("ya", "w_branch_a"), ("yb", "w_branch_b")):
        for i in range(2):
            unit(f"{n}{i}", WA, 4, [(arr, 512 * i, 512)])
    for i in range(4):
        unit(f"m{i}", D, 4, [("w_merge", 512 * i, 512)])
    for i in range(2):
        unit(f"wo{i}", D, 4, [("w_out", 512 * i, 512)])
    for i in range(2):
        unit(f"e{i}", D_PLE, 2, [("w_ple", 512 * i, 512)])
    for i in range(2):
        unit(f"pg{i}", D, 4, [("w_ple_gate", 512 * i, 512)])
    unit("sq", D, 4, [(w2, O2_Q, 512)])
    unit("skv", D, 8, [(w2, O2_KV, 256)])
    unit("ql", D, 4, [(w2, O2_QL, QR)])
    unit("kvl", D, 4, [(w2, O2_KVL, KVR + MR)])
    for i in range(2):
        unit(f"uq{i}", QR, 3, [("w_uq_2", 384 * i, 384)])
    for i in range(2):
        unit(f"ukv{i}", KVR, 2, [("w_ukv_2", 512 * i, 512)])
    for n, arr in (("za", "w_o_swa_2"), ("zb", "w_o_mla_2")):
        for i in range(2):
            unit(f"{n}{i}", WA, 4, [(arr, 512 * i, 512)])
    for i in range(4):
        unit(f"n{i}", D, 4, [(w2, O2_GA + 512 * i, 512)])
    for i in range(2):
        unit(f"wp{i}", D, 4, [("w_out_2", 512 * i, 512)])
    for i in range(DFF // 256):
        unit(f"f{i}", D, 4, [("w_gate_2", 256 * i, 256), ("w_up_2", 256 * i, 256)])
    unit("down", DFF, 2, [("w_down_2", 0, D)])
    return chunks, units


CHUNKS, UNITS = plan_weights()
LAST_OF = {f + n - 1: name for name, (f, n, _, _) in UNITS.items()}


class Attn:

    def __init__(self, name, index, keys):
        self.name, self.index = name, index
        self.units = [(b, h) for b in range(NB) for h in range(H)]
        self.keys = keys


ATT = {
    "fox": Attn("fox", 0, lambda b: (0, b + 1)),
    "dsa": Attn("dsa", 1, lambda b: (0, b + 1)),
    "swa": Attn("swa", 2, lambda b: (max(b - 1, 0), b + 1)),
    "mla": Attn("mla", 3, lambda b: (0, b + 1)),
}
NU = NB * H


def plan_banks():
    count = [0] * 8
    use = {}

    def fill(stage, banks):
        use[stage] = []
        for b in banks:
            use[stage].append((b, count[b]))
            count[b] += 1

    four = [0, 1, 2, 3]

    def attention(name):
        a = ATT[name]
        use[name + ".l"], use[name + ".t"], use[name + ".o"] = [], [], []
        for i, (b, h) in enumerate(a.units):
            use[name + ".l"].append((4 + i % 2, count[4 + i % 2]))
            count[4 + i % 2] += 1
            use[name + ".t"].append((6 + i % 2, count[6 + i % 2]))
            count[6 + i % 2] += 1
        for b in range(NB):
            use[name + ".o"].append((b, count[b]))
            count[b] += 1

    fill("qi", four); fill("norm1", [7, 6]); fill("sm", four); fill("qa", four)
    fill("t.qi", [4, 5, 6, 7]); fill("t.ki", [4])
    fill("idx", [4 + i % 4 for i in range(24)])
    fill("t.qa", [4, 5, 6, 7]); fill("t.ka", [4]); fill("cum", [5])
    fill("qb", four); fill("kb", four); fill("vb", four)
    attention("fox"); attention("dsa")
    fill("ga", four); fill("gb", four)
    fill("t.u", [4 + i % 4 for i in range(8)])
    for n in ("ya0", "ya1", "yb0", "yb1", "m0", "m1", "m2", "m3", "wo0", "wo1", "e0"):
        fill(n, four)
    fill("norm2", [7]); fill("e1", four); fill("pg0", four); fill("pg1", four)
    fill("norm3", [7])
    fill("sq", four); fill("norm4", [7, 6]); fill("skv", four)
    fill("t.sq", [4, 5, 6, 7]); fill("t.sk", [4, 5])
    attention("swa")
    fill("ql", four); fill("kvl", four)
    fill("t.cq", [4, 5, 6]); fill("t.ck", [7, 4])
    for i in range(2):
        fill(f"uq{i}", four); fill(f"t.mq{i}", [4, 5, 6, 7])
    for i in range(2):
        fill(f"ukv{i}", four); fill(f"t.mk{i}", [4, 5, 6, 7])
    attention("mla")
    fill("t.v", [4 + i % 4 for i in range(8)])
    for n in ("za0", "za1", "zb0", "zb1", "n0", "n1", "n2", "n3", "wp0", "wp1"):
        fill(n, four)
    fill("f0", four); fill("norm5", [7])
    for i in range(1, DFF // 256):
        fill(f"f{i}", four)
    fill("xr", list(range(8))); fill("down", list(range(8)))
    return use


USE = plan_banks()


def build(nc, dram, out):
    ctx = ExitStack()
    with ctx:
        def sb(name, shape, dt=F32):
            return ctx.enter_context(nc.sbuf_tensor(name, shape, dt))

        def sem(name):
            return ctx.enter_context(nc.semaphore(name))

        def phase(items):
            with ExitStack() as st:
                return [st.enter_context(nc.sbuf_tensor(n, s, d)) for n, s, d in items]

        w_raw = sb("w_raw", [P, 2, CH])
        w_hi = sb("w_hi", [P, 2, CH], F32R)
        w_lo = sb("w_lo", [P, 2, CH], F32R)
        xT = sb("xT", [P, KD, S])
        aH = sb("aH", [P, KD, S], F32R)
        aL = sb("aL", [P, KD, S], F32R)
        rB = sb("rB", [P, S])
        ssum = sb("ssum", [P, S])
        sq = sb("sq", [P, 2, S])
        rT = sb("rT", [P, NB])
        ident = sb("ident", [P, P])
        ident16 = sb("ident16", [P, P], BF16)
        diag16 = sb("diag16", [P, P], BF16)
        ones = sb("ones", [P, P])
        gv = sb("gv", [P, GV_W])
        mx = sb("mx", [P, NU])
        nbias = sb("nbias", [P, NU])
        sums = sb("sums", [P, NU])
        rsum = sb("rsum", [P, NU])
        m8 = sb("m8", [P, 3, 8])
        snk = sb("snk", [P, 2, H])
        bfg = sb("bfg", [P, H])
        lf = sb("lf", [P, 4, NB * H])
        qs = sb("qs", [P, 2, H])

        (tm, qiT, qaT, qbT, kbT, vb, cB, sm, rp, sc, sp, _, cst, pT, kT, cT) = phase([
            ("tm", [P, NB, S], F32), ("qiT", [P, NB, S], F32), ("qaT", [P, NB, S], F32),
            ("qbT", [P, NB, S], F32), ("kbT", [P, NB, S], F32), ("vb", [P, NB, S], F32),
            ("cB", [P, H, S], F32), ("sm", [P, NB, SM_W], F32), ("rp", [P, 2, 256], F32),
            ("sc", [P, 9 * P], F32), ("sp", [P, 3, S], F32), ("pad_a", [P, 64], F32),
            ("cst", [P, CST_W - P], F32), ("pT", [P, 2, S], F32),
            ("kT", [P, 2, S], F32), ("cT", [H, S], F32)])
        (_, _, _, _, _, _, _, _, _, _, _, _, _, kd) = phase([
            ("q0", [P, NB, S], F32), ("q1", [P, NB, S], F32), ("q2", [P, NB, S], F32),
            ("q3", [P, NB, S], F32), ("q4", [P, NB, S], F32), ("q5", [P, NB, S], F32),
            ("q6", [P, H, S], F32), ("q7", [P, NB, SM_W], F32), ("q8", [P, 2, 256], F32),
            ("q9", [P, 9 * P], F32), ("q10", [P, 3, S], F32), ("pad_q", [P, 64], F32),
            ("q12", [P, CST_W - P], F32), ("kd", [P, 2, NB, 2, DH], F32)])
        (yA, yB, uH, uL, sg, tmp, pH, pL, _, _, pr) = phase([
            ("yA", [P, KD, S], F32), ("yB", [P, KD, S], F32), ("uH", [P, KD, S], F32R),
            ("uL", [P, KD, S], F32R), ("sg", [P, 2, S], F32), ("tmp", [P, 2, S], F32),
            ("pH", [P, 2, S], F32R), ("pL", [P, 2, S], F32R), ("pad_b", [P, 64], F32),
            ("b9", [P, CST_W - P], F32), ("pr", [P, 2, S], F32)])
        (tm2, sqT, skv, skT, mqT, mkT, mv, oA, oB, _, _, sp2, pT2) = phase([
            ("tm2", [P, NB, S], F32), ("sqT", [P, NB, S], F32), ("skv", [P, NB, 256], F32),
            ("skT", [P, 2, S], F32), ("mqT", [P, H, S], F32), ("mkT", [P, H, S], F32),
            ("mv", [P, NB, H, DH], F32), ("oA", [P, NB, S], F32), ("oB", [P, NB, S], F32),
            ("pad_c", [P, 64], F32), ("c9", [P, CST_W - P], F32), ("sp2", [P, 3, S], F32),
            ("pT2", [P, 2, S], F32)])
        (ql, cqH, cqL, kvl, _, ckH, ckL) = phase([
            ("ql", [P, NB, QR], F32), ("cqH", [P, 3, S], F32R), ("cqL", [P, 3, S], F32R),
            ("kvl", [P, NB, KVR + MR], F32), ("pad_d", [P, 384 + 40 * 256 + 2048], F32),
            ("ckH", [P, 2, S], F32R), ("ckL", [P, 2, S], F32R)])
        (_, mk) = phase([("e0", [P, NB, QR], F32), ("mk", [P, NB, 4, MQK], F32)])
        (_, _, _, _, _, kd2) = phase([
            ("h0", [P, 64 * 256], F32), ("h1", [P, 16 * 256], F32), ("pad_h", [P, 64], F32),
            ("h3", [P, CST_W - P], F32), ("h4", [P, 3, S], F32), ("kd2", [P, NB, 2, P], F32)])
        (uH2, uL2, yA2, yB2, _, sg2, tmp2) = phase([
            ("uH2", [P, KD, S], F32R), ("uL2", [P, KD, S], F32R), ("yA2", [P, KD, S], F32),
            ("yB2", [P, KD, S], F32), ("i4", [P, 16 * 256], F32), ("sg2", [P, 2, S], F32),
            ("tmp2", [P, 2, S], F32)])
        NF = DFF // P
        (fH, fL, fg, fu, gfin) = phase([
            ("fH", [P, NF, S], F32R), ("fL", [P, NF, S], F32R), ("fg", [P, 2, S], F32),
            ("fu", [P, 2, S], F32), ("gfin", [P, D], F32)])
        xr = xT[:, :, :].rearrange("p a b -> p (a b)").rearrange("p (b d) -> p b d", b=NB)
        oT, eT = yB, yA

        def kdT(which):
            return kT[:, which, :]

        def tab(name):
            o, w = _C[name]
            return cst[:, o - P:o - P + w]

        def rope_tab(name, half):
            return tab(name).rearrange("p (b f) -> p b f", b=NB)

        bank = [ctx.enter_context(nc.psum_tensor(f"bank{i}", [P, S], F32)) for i in range(8)]
        filled = [sem(f"filled{i}") for i in range(8)]
        emptied = [sem(f"emptied{i}") for i in range(8)]

        w_landed = [sem(f"w_landed{i}") for i in range(2)]
        w_hi_ready, w_lo_ready, w_used = sem("w_hi_ready"), sem("w_lo_ready"), sem("w_used")
        x_landed = [sem(f"x_landed{i}") for i in range(4)]
        cst_landed, small_landed, p_landed = sem("cst_landed"), sem("small_landed"), sem("p_landed")
        ones_ready, half_ready = sem("ones_ready"), sem("half_ready")
        sq_ready, sum_ready, rb_ready, rt_ready = sem("sq_ready"), sem("sum_ready"), sem("rb_ready"), sem("rt_ready")
        a_hi_ready, a_lo_ready = sem("a_hi_ready"), sem("a_lo_ready")
        roped, kd_ready = sem("roped"), sem("kd_ready")
        logf_ready, cum_stored, cum_landed = sem("logf_ready"), sem("cum_stored"), sem("cum_landed")
        lf_in, lf_ln = sem("lf_in"), sem("lf_ln")
        scored, idx_done, chosen = sem("scored"), sem("idx_done"), sem("chosen")
        qb_scaled = sem("qb_scaled")
        biased, exped, pv_done = sem("biased"), sem("exped"), sem("pv_done")
        att_out, sink_exp = sem("att_out"), sem("sink_exp")
        u_ready, u_hi_ready, u_lo_ready = sem("u_ready"), sem("u_hi_ready"), sem("u_lo_ready")
        gate_ready, gate_lin = sem("gate_ready"), sem("gate_lin")
        sg_ready, z_ready = sem("sg_ready"), sem("z_ready")
        p_hi_ready, p_lo_ready = sem("p_hi_ready"), sem("p_lo_ready")
        x_new, y_ready = sem("x_new"), sem("y_ready")
        ql_sq, ql_r, ql_scaled = sem("ql_sq"), sem("ql_r"), sem("ql_scaled")
        c_hi_ready, c_lo_ready = sem("c_hi_ready"), sem("c_lo_ready")
        mk_ready = sem("mk_ready")
        ff_act, ff_prod, ff_hi, ff_lo = sem("ff_act"), sem("ff_prod"), sem("ff_hi"), sem("ff_lo")
        fin_ready, fin_sq, fin_rms, stored = sem("fin_ready"), sem("fin_sq"), sem("fin_rms"), sem("stored")
        dve_step, act_step = sem("dve_step"), sem("act_step")

        cum_dram = nc.dram_tensor("cum_scratch", (H, S), F32, kind="Internal").ap()

        def wait_filled(eng, stage, i):
            b, n = USE[stage][i]
            eng.wait_ge(filled[b], n + 1)

        def wait_emptied(eng, stage, i):
            b, n = USE[stage][i]
            eng.wait_ge(emptied[b], n + 1)

        def bank_of(stage, i):
            return bank[USE[stage][i][0]]

        def empties(ins, stage, i):
            ins.then_inc(emptied[USE[stage][i][0]], 1)

        def wait_used(eng, c):
            if c in LAST_OF:
                wait_filled(eng, LAST_OF[c], len(USE[LAST_OF[c]]) - 1)
            else:
                eng.wait_ge(w_used, sum(1 for i in range(c + 1) if i not in LAST_OF))

        def turn(eng, copy, a, i, pt):
            b, h = a.units[i]
            k0, k1 = a.keys(b)
            n = (k1 - k0) * P
            if i >= 2:
                wait_pv(eng, a, i - 2)
            wait_filled(eng, a.name + ".t", i)
            empties(copy(out=pt[:, i % 2, 0:n], in_=bank_of(a.name + ".t", i)[:, 0:n]), a.name + ".t", i)

        def wait_pv(eng, a, i):
            b, h = a.units[i]
            if h == H - 1:
                wait_filled(eng, a.name + ".o", b)
            else:
                eng.wait_ge(pv_done, a.index * NB * (H - 1) + b * (H - 1) + h + 1)

        def w_view(buf, c):
            per, n, _ = CHUNKS[c]
            return buf[:, c % 2, 0:per * n].rearrange("p (k n) -> p k n", n=n)

        landed, total = [], [0, 0]
        for c, (_, _, ps) in enumerate(CHUNKS):
            total[c % 2] += 16 * len(ps)
            landed.append(total[c % 2])

        block = ctx.enter_context(nc.Block())

        @block.sync
        def _(sp_):
            sp_.dma_start(gv[:], dram["gains"]).then_inc(small_landed, 16)
            xv = dram["xT"].rearrange("(k p) t -> p k t", p=P)

            def load(c):
                if c >= 2:
                    sp_.wait_ge(w_hi_ready, c - 1)
                    sp_.wait_ge(w_lo_ready, c - 1)
                per, n, ps = CHUNKS[c]
                v = w_view(w_raw, c)
                for arr, r0, c0, w, off in ps:
                    src = dram[arr][0, r0:r0 + per * P, c0:c0 + w].rearrange("(k p) n -> p k n", p=P)
                    sp_.dma_start(v[:, :, off:off + w], src).then_inc(w_landed[c % 2], 16)

            for i in range(4):
                sp_.dma_start(xT[:, 2 * i:2 * i + 2, :], xv[:, 2 * i:2 * i + 2, :]).then_inc(x_landed[i], 16)
                if i == 0:
                    load(0)
            sp_.dma_start(ident[:], dram["cst"][:, 0:P]).then_inc(cst_landed, 16)
            sp_.dma_start(cst[:], dram["cst"][:, P:]).then_inc(cst_landed, 16)
            sp_.dma_start(bfg[:], dram["b_forget"].broadcast_to([P, H])).then_inc(small_landed, 16)
            sp_.dma_start(snk[:, 0, :], dram["swa_sinks_2"].broadcast_to([P, H])).then_inc(small_landed, 16)
            for c in range(1, len(CHUNKS)):
                load(c)
                if c == UNITS["vb"][0]:
                    wait_emptied(sp_, "cum", 0)
                    sp_.dma_start(cum_dram, cT[:, :]).then_inc(cum_stored, 16)
                    sp_.wait_ge(cum_stored, 16)
                    sp_.dma_start(cB[:], cum_dram.rearrange("(o h) k -> o h k", o=1).broadcast_to([P, H, S])).then_inc(cum_landed, 16)
                if c == UNITS["m2"][0]:
                    wait_filled(sp_, "dsa.o", NB - 1)
                    sp_.dma_start(pr[:], dram["pT"].rearrange("(k p) t -> p k t", p=P)).then_inc(p_landed, 16)
                if c == UNITS["f2"][0]:
                    sp_.dma_start(gfin[:], dram["final_norm_g_2"].broadcast_to([P, D])).then_inc(small_landed, 16)
            for b in range(NB):
                sp_.wait_ge(fin_ready, b + 1)
                sp_.dma_start(out[0, b * P:(b + 1) * P, :], xr[:, b, :]).then_inc(stored, 16)
            sp_.wait_ge(stored, 16 * NB)

        @block.gpsimd
        def _(pool):
            pool.memset(ones[:], 1.0).then_inc(ones_ready, 1)
            next_chunk = [0]

            def lo_through(c_end):
                for c in range(next_chunk[0], min(c_end + 1, len(CHUNKS))):
                    n = CHUNKS[c][0] * CHUNKS[c][1]
                    pool.wait_ge(w_hi_ready, c + 1)
                    pool.tensor_tensor(out=w_lo[:, c % 2, 0:n], in0=w_raw[:, c % 2, 0:n],
                                       in1=w_hi[:, c % 2, 0:n].bitcast(F32), op=ALU.subtract).then_inc(w_lo_ready, 1)
                    next_chunk[0] = c + 1

            for u, t in (("qb", qbT), ("kb", kbT)):
                lo_through(UNITS[u][0] + UNITS[u][1] + 1)
                pool.wait_ge(rb_ready, 1)
                for j in range(NB):
                    wait_emptied(pool, u, j)
                    pool.tensor_tensor(out=t[:, j, :], in0=t[:, j, :], in1=rB[:], op=ALU.mult).then_inc(qb_scaled, 1)
            lo_through(len(CHUNKS) - 1)

        @block.scalar
        def _(act):
            nxt = [0]

            def hi_through(c_end):
                for c in range(nxt[0], min(c_end + 1, len(CHUNKS))):
                    n = CHUNKS[c][0] * CHUNKS[c][1]
                    act.wait_ge(w_landed[c % 2], landed[c])
                    if c >= 2:
                        wait_used(act, c - 2)
                    act.activation(w_hi[:, c % 2, 0:n], w_raw[:, c % 2, 0:n], ACT.Copy).then_inc(w_hi_ready, 1)
                    nxt[0] = c + 1

            def ahead(unit):
                first, n, _, _ = UNITS[unit]
                hi_through(first + n)

            def evac(stage, i, dst, src=None, scale=1.0):
                wait_filled(act, stage, i)
                src = bank_of(stage, i)[:] if src is None else src
                empties(act.activation(dst, src, ACT.Copy, scale=scale), stage, i)

            def square(n, j, src):
                base = 8 * (n - 1)
                if base + j >= 2:
                    act.wait_ge(sum_ready, base + j - 1)
                act.activation(sq[:, j % 2, :], src, ACT.Square).then_inc(sq_ready, 1)

            def rms(n, tm_too):
                wait_filled(act, f"norm{n}", 0)
                if tm_too:
                    wait_filled(act, f"norm{n}", 1)
                empties(act.activation(rB[:], bank_of(f"norm{n}", 0)[:], ACT.Sqrt, scale=1.0 / D, bias=EPS),
                        f"norm{n}", 0)
                if tm_too:
                    empties(act.activation(rT[:], bank_of(f"norm{n}", 1)[:, 0:NB], ACT.Sqrt, scale=1.0 / D, bias=EPS),
                            f"norm{n}", 1)

            def exps(name, sp):
                a = ATT[name]
                scale = MQK ** -0.5 if name == "mla" else DH ** -0.5
                pt = pT if a.index < 2 else pT2
                for i in range(NU + 2):
                    if i < NU:
                        b, h = a.units[i]
                        k0, k1 = a.keys(b)
                        s = sp[:, i % 3, 0:(k1 - k0) * P]
                        act.wait_ge(biased, a.index * NU + i + 1)
                        act.activation(s, s, ACT.Exp, bias=nbias[:, i:i + 1], scale=scale,
                                       accum_out=sums[:, i:i + 1]).then_inc(exped, 1)
                        if name == "swa" and h == H - 1:
                            act.wait_ge(sink_exp, 2 * b + 1)
                            act.activation(qs[:, 0, :], qs[:, 0, :], ACT.Exp).then_inc(sink_exp, 1)
                    if i >= 2 and i % 2 == 1:
                        turn(act, act.copy, a, i - 2, pt)

            act.wait_ge(small_landed, 16)
            for j in range(KD):
                act.wait_ge(x_landed[j // 2], 16)
                act.activation(aH[:, j, :], xT[:, j, :], ACT.Copy, scale=gv[:, GV["pre"] + j:GV["pre"] + j + 1]).then_inc(a_hi_ready, 1)
                square(1, j, xT[:, j, :])
                if j == 1:
                    hi_through(0)
            hi_through(1)
            rms(1, True)
            act.wait_ge(rt_ready, 1)
            ahead("qi")
            for b in range(NB):
                evac("qi", b, tm[:, b, :], scale=rT[:, b:b + 1])
            ahead("sm")
            for b in range(NB):
                evac("sm", b, sm[:, b, :], src=bank_of("sm", b)[:, 0:SM_W], scale=rT[:, b:b + 1])
            act.wait_ge(lf_in, 1)
            act.activation(lf[:, 1, :], lf[:, 1, :], ACT.Exp).then_inc(act_step, 1)
            act.wait_ge(act_step, 1)
            act.activation(lf[:, 1, :], lf[:, 1, :], ACT.Ln, bias=1.0).then_inc(lf_ln, 1)
            ahead("qa")
            for b in range(NB):
                if b == 0:
                    wait_filled(act, "t.qi", NB - 1)
                evac("qa", b, tm[:, b, :], scale=rT[:, b:b + 1])
            hi_through(UNITS["qa"][0] + UNITS["qa"][1] + 1)
            for i in range(24):
                h, b = i // 3, 1 + i % 3
                nk = (b + 1) * P
                if i >= 3:
                    act.wait_ge(idx_done, i - 2)
                wait_filled(act, "idx", i)
                empties(act.activation(sp[:, i % 3, 0:nk], bank_of("idx", i)[:, 0:nk], ACT.Relu), "idx", i)
            ahead("qb")
            evac("cum", 0, cT[:, :], src=bank_of("cum", 0)[0:H, :], scale=-8.0)
            for u, t in (("qb", qbT), ("kb", kbT)):
                ahead(u)
                for j in range(NB):
                    evac(u, j, t[:, j, :])
            ahead("vb")
            for b in range(NB):
                evac("vb", b, vb[:, b, :], scale=rT[:, b:b + 1])
            hi_through(UNITS["vb"][0] + UNITS["vb"][1] + 1)
            exps("fox", sp)
            exps("dsa", sp)
            for n, (u, g) in enumerate((("ga", qaT), ("gb", qbT))):
                ahead(u)
                for j in range(NB):
                    wait_emptied(act, u, j)
                    act.activation(g[:, j, :], g[:, j, :], ACT.Silu).then_inc(gate_ready, 1)
            for i in range(8):
                wait_emptied(act, "t.u", i)
                act.activation(uH[:, i, :], tmp[:, i % 2, :], ACT.Copy).then_inc(u_hi_ready, 1)

            def mix(first, names, y, zH, sg, base, u_done):
                for n, (u, t) in enumerate(((names[0] + "0", y[0]), (names[0] + "1", y[0]),
                                            (names[1] + "0", y[1]), (names[1] + "1", y[1]))):
                    ahead(u)
                    for j in range(NB):
                        evac(u, j, t[:, 4 * (n % 2) + j, :])
                for n in range(4):
                    ahead(f"{names[2]}{n}")
                    for j in range(NB):
                        wait_emptied(act, f"{names[2]}{n}", j)
                        act.activation(sg[:, j % 2, :], sg[:, j % 2, :], ACT.Sigmoid).then_inc(sg_ready, 1)
                        if n >= 2:
                            t = 4 * (n - 2) + j
                            if t >= 1:
                                hi_z(t - 1, y, zH, base)
                hi_z(7, y, zH, base)

            def hi_z(t, y, zH, base):
                act.wait_ge(z_ready, base + t + 1)
                act.activation(zH[:, t, :], y[0][:, t, :], ACT.Copy).then_inc(u_hi_ready, 1)

            mix(None, ("ya", "yb", "m"), (yA, yB), uH, sg, 0, None)
            for j in range(2):
                act.wait_ge(p_landed, 16)
                act.activation(pH[:, j, :], pr[:, j, :], ACT.Copy).then_inc(p_hi_ready, 1)
            for n in range(2):
                ahead(f"wo{n}")
                for j in range(NB):
                    t = 4 * n + j
                    evac(f"wo{n}", j, oT[:, t, :])
                    wait_emptied(act, f"wo{n}", j)
                    square(2, t, oT[:, t, :])
            rms(2, False)
            ahead("e0")
            for j in range(NB):
                evac("e0", j, eT[:, j, :])
            for j in range(KD):
                act.wait_ge(x_new, j + 1)
                act.activation(aH[:, j, :], xT[:, j, :], ACT.Copy).then_inc(a_hi_ready, 1)
            ahead("e1")
            for j in range(NB):
                evac("e1", j, eT[:, 4 + j, :])
            for n in range(2):
                ahead(f"pg{n}")
                for j in range(NB):
                    t = 4 * n + j
                    if t >= 2:
                        act.wait_ge(y_ready, t - 1)
                    wait_filled(act, f"pg{n}", j)
                    empties(act.activation(sg[:, t % 2, :], bank_of(f"pg{n}", j)[:], ACT.Sigmoid), f"pg{n}", j)
                    if t >= 1:
                        act.wait_ge(y_ready, t)
                        square(3, t - 1, oT[:, t - 1, :])
            act.wait_ge(y_ready, 8)
            square(3, 7, oT[:, 7, :])
            rms(3, False)
            for j in range(KD):
                act.wait_ge(x_new, 8 + j + 1)
                act.activation(aH[:, j, :], xT[:, j, :], ACT.Copy, scale=gv[:, GV["mix"] + j:GV["mix"] + j + 1]).then_inc(a_hi_ready, 1)
                square(4, j, xT[:, j, :])
            hi_through(UNITS["sq"][0] + 1)
            rms(4, True)
            act.wait_ge(rt_ready, 2)
            ahead("sq")
            for b in range(NB):
                evac("sq", b, tm2[:, b, :], scale=rT[:, b:b + 1])
            ahead("skv")
            for b in range(NB):
                evac("skv", b, skv[:, b, :], src=bank_of("skv", b)[:, 0:256], scale=rT[:, b:b + 1])
            hi_through(UNITS["skv"][0] + UNITS["skv"][1] + 1)
            exps("swa", sp2)
            for n, (u, t, w) in enumerate((("ql", ql, QR), ("kvl", kvl, KVR))):
                ahead(u)
                full = CHUNKS[UNITS[u][0]][1]
                for b in range(NB):
                    evac(u, b, t[:, b, :], src=bank_of(u, b)[:, 0:full], scale=rT[:, b:b + 1])
                for b in range(NB):
                    wait_emptied(act, u, b)
                    if 4 * n + b >= 2:
                        act.wait_ge(ql_sq, 4 * n + b - 1)
                    act.activation(sq[:, b % 2, 0:w], t[:, b, 0:w], ACT.Square,
                                   accum_out=qs[:, n, b:b + 1]).then_inc(ql_sq, 1)
                act.wait_ge(ql_sq, 4 * n + 4)
                act.activation(qs[:, n, 4:8], qs[:, n, 0:4], ACT.Sqrt, scale=1.0 / w, bias=EPS).then_inc(ql_r, 1)
            for stage, tiles, dst, g, base in (("t.cq", 3, cqH, "q", 0), ("t.ck", 2, ckH, "kv", 3)):
                for j in range(tiles):
                    wait_filled(act, stage, j)
                    act.activation(dst[:, j, :], bank_of(stage, j)[:], ACT.Copy,
                                   scale=gv[:, GV[g] + j:GV[g] + j + 1]).then_inc(c_hi_ready, 1)
            for i in range(2):
                ahead(f"uq{i}")
                if i == 1:
                    wait_filled(act, "t.mq0", 3)
                for b in range(NB):
                    evac(f"uq{i}", b, ql[:, b, :], src=bank_of(f"uq{i}", b)[:, 0:QR])
            for i in range(2):
                ahead(f"ukv{i}")
                if i == 1:
                    wait_filled(act, "t.mk0", 3)
                for b in range(NB):
                    src = bank_of(f"ukv{i}", b)[:].rearrange("p (h d) -> p h d", h=4)
                    wait_filled(act, f"ukv{i}", b)
                    act.activation(mk[:, b, :, 0:DH], src[:, :, 0:DH], ACT.Copy).then_inc(mk_ready, 1)
                    empties(act.activation(mv[:, b, 4 * i:4 * i + 4, :], src[:, :, DH:2 * DH], ACT.Copy), f"ukv{i}", b)
            hi_through(UNITS["ukv1"][0] + UNITS["ukv1"][1] + 1)
            exps("mla", sp2)
            for i in range(8):
                wait_filled(act, "t.v", i)
                act.activation(uH2[:, i, :], bank_of("t.v", i)[:], ACT.Copy).then_inc(u_hi_ready, 1)
            mix(None, ("za", "zb", "n"), (yA2, yB2), uH2, sg2, 8, None)
            for j in range(KD):
                if j % 4 == 0:
                    ahead(f"wp{j // 4}")
                wait_emptied(act, f"wp{j // 4}", j % 4)
                act.activation(aH[:, j, :], xT[:, j, :], ACT.Copy, scale=gv[:, GV["ffn"] + j:GV["ffn"] + j + 1]).then_inc(a_hi_ready, 1)
                square(5, j, xT[:, j, :])
            hi_through(UNITS["f0"][0] + 1)
            rms(5, False)
            for f in range(DFF // 256):
                ahead(f"f{f}")
                for j in range(2):
                    wait_emptied(act, f"f{f}", j)
                    act.activation(fg[:, j, :], fg[:, j, :], ACT.Silu).then_inc(ff_act, 1)
                for j in range(2):
                    t = 2 * f + j
                    act.wait_ge(ff_prod, t + 1)
                    act.activation(fH[:, t, :], fg[:, j, :], ACT.Copy).then_inc(ff_hi, 1)
            for i in range(0, 8, 2):
                if i == 0:
                    wait_filled(act, "xr", 7)
                evac("xr", i, xr[:, i // 2, 512 * (i % 2):512 * (i % 2) + 512])
            hi_through(len(CHUNKS) - 1)
            for b in range(NB):
                act.wait_ge(fin_sq, b + 1)
                act.activation(sq[:, :, :].rearrange("p a b -> p (a b)"), xr[:, b, :], ACT.Square,
                               accum_out=qs[:, 0, b:b + 1]).then_inc(act_step, 1)
                act.wait_ge(act_step, 2 + 2 * b)
                act.activation(qs[:, 1, b:b + 1], qs[:, 0, b:b + 1], ACT.Sqrt, scale=1.0 / D, bias=EPS).then_inc(act_step, 1)


        @block.vector
        def _(dve):
            steps, ropes = [0], [0]

            def link(ins):
                steps[0] += 1
                ins.then_inc(dve_step, 1)
                dve.wait_ge(dve_step, steps[0])

            def mult(o, a, b):
                return dve.tensor_tensor(out=o, in0=a, in1=b, op=ALU.mult)

            def add_sq(n, j):
                base = 8 * (n - 1)
                dve.wait_ge(sq_ready, base + j + 1)
                if j == 0:
                    if n > 1:
                        wait_filled(dve, f"norm{n - 1}", len(USE[f"norm{n - 1}"]) - 1)
                    dve.tensor_copy(ssum[:], sq[:, 0, :]).then_inc(sum_ready, 1)
                else:
                    dve.wait_ge(sum_ready, base + j)
                    dve.tensor_tensor(out=ssum[:], in0=ssum[:], in1=sq[:, j % 2, :], op=ALU.add).then_inc(sum_ready, 1)

            def rms(n, tm_too):
                wait_emptied(dve, f"norm{n}", 0)
                dve.reciprocal(rB[:], rB[:]).then_inc(rb_ready, 1)
                if tm_too:
                    wait_emptied(dve, f"norm{n}", 1)
                    dve.reciprocal(rT[:], rT[:]).then_inc(rt_ready, 1)

            def rope(x, shape, half, cos, sin, t0, t1):
                x1, x2 = x[..., 0:half], x[..., half:2 * half]
                mult(t0, x2, sin)
                mult(t1, x1, sin)
                mult(x1, x1, cos)
                link(mult(x2, x2, cos))
                dve.tensor_tensor(out=x1, in0=x1, in1=t0, op=ALU.subtract)
                dve.tensor_tensor(out=x2, in0=x2, in1=t1, op=ALU.add).then_inc(roped, 1)
                ropes[0] += 1
                dve.wait_ge(roped, ropes[0])

            def rope_blocks(x, heads, half, which, rp):
                cos, sin = (rope_tab(n + which, half).rearrange("p b (o f) -> p b o f", o=1)
                            .broadcast_to([P, NB, heads, half]) for n in ("cos", "sin"))
                n = NB * heads * half
                t0, t1 = (rp[:, i, 0:n].rearrange("p (b h f) -> p b h f", b=NB, h=heads) for i in range(2))
                rope(x, None, half, cos, sin, t0, t1)

            def rope_block(x, b, heads, half, which, rp):
                cos, sin = (rope_tab(n + which, half)[:, b:b + 1, :].broadcast_to([P, heads, half])
                            for n in ("cos", "sin"))
                n = heads * half
                t0, t1 = (rp[:, i, 0:n].rearrange("p (h f) -> p h f", h=heads) for i in range(2))
                rope(x, None, half, cos, sin, t0, t1)

            def evac(stage, i, dst, src=None):
                wait_filled(dve, stage, i)
                empties(dve.tensor_copy(dst, bank_of(stage, i)[:] if src is None else src), stage, i)

            def softmax(name, sp, pt, att, k_bias):
                a = ATT[name]
                scale = MQK ** -0.5 if name == "mla" else DH ** -0.5
                for i in range(NU + 4):
                    if i < NU:
                        b, h = a.units[i]
                        k0, k1 = a.keys(b)
                        n = (k1 - k0) * P
                        if i >= 3:
                            wait_filled(dve, name + ".t", i - 3)
                        wait_filled(dve, name + ".l", i)
                        empties(dve.tensor_tensor_reduce(
                            out=sp[:, i % 3, 0:n], in0=bank_of(name + ".l", i)[:, 0:n], in1=k_bias(b, h),
                            scale=1.0, scalar=-3e38, op0=ALU.add, op1=ALU.max, accum_out=mx[:, i:i + 1]),
                            name + ".l", i)
                        wait_emptied(dve, name + ".l", i)
                        if name == "swa":
                            dve.tensor_scalar(nbias[:, i:i + 1], mx[:, i:i + 1], -scale, snk[:, 1, h:h + 1],
                                              ALU.mult, ALU.min).then_inc(biased, 1)
                            if h == H - 1:
                                dve.wait_ge(biased, a.index * NU + i + 1)
                                dve.tensor_tensor(out=qs[:, 0, :], in0=nbias[:, 8 * b:8 * b + 8], in1=snk[:, 0, :],
                                                  op=ALU.add).then_inc(sink_exp, 1)
                        else:
                            dve.tensor_scalar(nbias[:, i:i + 1], mx[:, i:i + 1], -scale, None,
                                              ALU.mult).then_inc(biased, 1)
                    if 2 <= i < NU + 2 and i % 2 == 0:
                        turn(dve, dve.tensor_copy, a, i - 2, pt)
                    if i >= 4 and (i - 4) % H == H - 1:
                        b = (i - 4) // H
                        cols = slice(H * b, H * b + H)
                        dve.wait_ge(exped, a.index * NU + H * b + H)
                        if name == "swa":
                            dve.wait_ge(sink_exp, 2 * b + 2)
                            link(dve.tensor_tensor(out=sums[:, cols], in0=sums[:, cols], in1=qs[:, 0, :], op=ALU.add))
                        link(dve.reciprocal(rsum[:, cols], sums[:, cols]))
                        wait_filled(dve, name + ".o", b)
                        empties(mult(att[:, b, :].rearrange("p (h d) -> p h d", h=H),
                                     bank_of(name + ".o", b)[:].rearrange("p (h d) -> p h d", h=H),
                                     rsum[:, cols].rearrange("p (h o) -> p h o", o=1).broadcast_to([P, H, DH])),
                                name + ".o", b)

            def mix(names, y, zH, zL, sg, base):
                def prod(q):
                    dve.wait_ge(sg_ready, 2 * base + q + 1)
                    if q < 8:
                        wait_emptied(dve, f"{names[0]}{q // 4}", q % 4)
                        link(mult(y[0][:, q, :], sg[:, q % 2, :], y[0][:, q, :]))
                        return
                    t = q - 8
                    wait_emptied(dve, f"{names[1]}{t // 4}", t % 4)
                    link(mult(y[1][:, t, :], sg[:, q % 2, :], y[1][:, t, :]))
                    dve.tensor_tensor(out=y[0][:, t, :], in0=y[0][:, t, :], in1=y[1][:, t, :],
                                      op=ALU.add).then_inc(z_ready, 1)

                def low(t):
                    dve.wait_ge(u_hi_ready, 2 * base + 8 + t + 1)
                    dve.tensor_tensor(out=zL[:, t, :], in0=y[0][:, t, :], in1=zH[:, t, :].bitcast(F32),
                                      op=ALU.subtract).then_inc(u_lo_ready, 1)

                for q in range(18):
                    if q < 16:
                        n, j = q // 4, q % 4
                        wait_filled(dve, f"{names[2]}{n}", j)
                        empties(mult(sg[:, q % 2, :], bank_of(f"{names[2]}{n}", j)[:], rB[:]), f"{names[2]}{n}", j)
                    if 1 <= q <= 16:
                        prod(q - 1)
                    if q >= 10:
                        low(q - 10)

            dve.wait_ge(cst_landed, 32)
            dve.tensor_copy(ident16[:], ident[:])
            dve.tensor_copy(diag16[:], tab("causal")[:, 3 * P:4 * P]).then_inc(half_ready, 1)
            dve.wait_ge(small_landed, 48)
            for j in range(KD):
                dve.wait_ge(a_hi_ready, j + 1)
                dve.scalar_tensor_tensor(out=aL[:, j, :], in0=xT[:, j, :], scalar=gv[:, GV["pre"] + j:GV["pre"] + j + 1],
                                         in1=aH[:, j, :].bitcast(F32), op0=ALU.mult, op1=ALU.subtract).then_inc(a_lo_ready, 1)
                add_sq(1, j)
            rms(1, True)
            tm4 = tm[:, :, :].rearrange("p b (h d) -> p b h d", h=H)
            for b in range(NB):
                wait_emptied(dve, "qi", b)
            rope_blocks(tm4, H, 8, "1", rp)
            for b in range(NB):
                wait_emptied(dve, "sm", b)
            for which, o in enumerate((SM_KI, SM_KA)):
                link_rope = sm[:, :, o:o + DH].rearrange("p b (h d) -> p b h d", h=1)
                rope_blocks(link_rope, 1, 8, "1", rp)
                for c in range(2):
                    ins = dve.tensor_copy(kd[:, which, :, c, :], sm[:, :, o:o + DH])
                ins.then_inc(kd_ready, 1)
            link(dve.tensor_scalar(sm[:, :, SM_WI:SM_WI + H], sm[:, :, SM_WI:SM_WI + H], (H ** -0.5) * (DH ** -0.5),
                                   None, ALU.mult))
            z = lf[:, 0, :].rearrange("p (b h) -> p b h", b=NB)
            link(dve.tensor_tensor(out=z, in0=sm[:, :, SM_FB:SM_FB + H],
                                   in1=bfg[:, :].rearrange("p (o h) -> p o h", o=1).broadcast_to([P, NB, H]), op=ALU.add))
            dve.scalar_tensor_tensor(out=lf[:, 1, :], in0=lf[:, 0, :], scalar=-1.0, in1=lf[:, 0, :],
                                     op0=ALU.mult, op1=ALU.min).then_inc(lf_in, 1)
            link(dve.tensor_scalar(lf[:, 2, :], lf[:, 0, :], 0.0, None, ALU.min))
            for j in range(NB):
                evac("t.qi", j, qiT[:, j, :])
            evac("t.ki", 0, kdT(0))
            dve.wait_ge(lf_ln, 1)
            dve.tensor_tensor(out=lf[:, 3, :], in0=lf[:, 2, :], in1=lf[:, 1, :], op=ALU.subtract).then_inc(logf_ready, 1)

            span = {1: (0, 2 * P), 2: (2 * P, 5 * P), 3: (5 * P, 9 * P)}
            for i in range(24):
                h, b = i // 3, 1 + i % 3
                lo, hi = span[b]
                dve_in = sp[:, i % 3, 0:hi - lo]
                w = sm[:, b, SM_WI + h:SM_WI + h + 1]
                wait_emptied(dve, "idx", i)
                if h == 0:
                    dve.tensor_scalar(sc[:, lo:hi], dve_in, w, None, ALU.mult).then_inc(idx_done, 1)
                else:
                    dve.wait_ge(idx_done, i - 2)
                    dve.scalar_tensor_tensor(out=sc[:, lo:hi], in0=dve_in, scalar=w, in1=sc[:, lo:hi],
                                             op0=ALU.mult, op1=ALU.add).then_inc(idx_done, 1)
                if i == 2:
                    for b in range(NB):
                        wait_emptied(dve, "qa", b)
                    rope_blocks(tm4, H, 8, "1", rp)
            dve.wait_ge(idx_done, 24)
            for b in range(1, NB):
                lo, hi = span[b]
                ins = dve.tensor_tensor(out=sc[:, hi - P:hi], in0=sc[:, hi - P:hi], in1=tab("causal")[:, 3 * P:4 * P],
                                        op=ALU.add)
            link(ins)
            for j in range(NB):
                evac("t.qa", j, qaT[:, j, :])
            evac("t.ka", 0, kdT(1))
            for r in range(TOPK // 8):
                for b in range(1, NB):
                    lo, hi = span[b]
                    ins = dve.max(out=m8[:, b - 1, :], in_=sc[:, lo:hi])
                link(ins)
                for b in range(1, NB):
                    lo, hi = span[b]
                    ins = dve.match_replace(out=sc[:, lo:hi], in_to_replace=m8[:, b - 1, :], in_values=sc[:, lo:hi],
                                            imm_value=TAKEN)
                link(ins)
            link(dve.tensor_scalar(sc[:], sc[:], TAKEN * 0.9, NEG, ALU.is_gt, ALU.mult))

            dve.wait_ge(cum_landed, 16)
            softmax("fox", sp, pT, tm, lambda b, h: cB[:, h, 0:(b + 1) * P])
            softmax("dsa", sp, pT, qiT,
                    lambda b, h: tab("causal")[:, 3 * P:4 * P] if b == 0 else sc[:, span[b][0]:span[b][1]])
            for u, g in (("ga", qaT), ("gb", qbT)):
                for j in range(NB):
                    wait_filled(dve, u, j)
                    empties(mult(g[:, j, :], bank_of(u, j)[:], rB[:]), u, j)
            for i in range(9):
                if i < 8:
                    g = (qaT, qbT)[i // 4]
                    if i >= 2:
                        dve.wait_ge(u_lo_ready, i - 1)
                    dve.wait_ge(gate_ready, i + 1)
                    wait_filled(dve, "t.u", i)
                    empties(mult(tmp[:, i % 2, :], bank_of("t.u", i)[:], g[:, i % 4, :]), "t.u", i)
                if i >= 1:
                    dve.wait_ge(u_hi_ready, i)
                    dve.tensor_tensor(out=uL[:, i - 1, :], in0=tmp[:, (i - 1) % 2, :],
                                      in1=uH[:, i - 1, :].bitcast(F32), op=ALU.subtract).then_inc(u_lo_ready, 1)
            mix(("ya", "yb", "m"), (yA, yB), uH, uL, sg, 0)
            for j in range(2):
                dve.wait_ge(p_hi_ready, j + 1)
                dve.tensor_tensor(out=pL[:, j, :], in0=pr[:, j, :], in1=pH[:, j, :].bitcast(F32),
                                  op=ALU.subtract).then_inc(p_lo_ready, 1)

            def residual(n, gname, after, gnext):
                for j in range(9):
                    if j < 8:
                        g = gv[:, GV[gname] + j:GV[gname] + j + 1]
                        link(dve.scalar_tensor_tensor(out=tmp[:, j % 2, :], in0=oT[:, j, :], scalar=g, in1=rB[:],
                                                      op0=ALU.mult, op1=ALU.mult))
                        dve.tensor_tensor(out=xT[:, j, :], in0=xT[:, j, :], in1=tmp[:, j % 2, :],
                                          op=ALU.add).then_inc(x_new, 1)
                    if j >= 1:
                        low_x(n, j - 1, gnext)
                        if after:
                            add_sq(after, j - 1)

            def low_x(n, j, gnext):
                dve.wait_ge(a_hi_ready, 8 * n + j + 1)
                g = 1.0 if gnext is None else gv[:, GV[gnext] + j:GV[gnext] + j + 1]
                dve.scalar_tensor_tensor(out=aL[:, j, :], in0=xT[:, j, :], scalar=g, in1=aH[:, j, :].bitcast(F32),
                                         op0=ALU.mult, op1=ALU.subtract).then_inc(a_lo_ready, 1)

            for j in range(8):
                add_sq(2, j)
            rms(2, False)
            dve.wait_ge(rb_ready, 2)
            residual(1, "post", None, None)
            for t in range(9):
                if t < 8:
                    wait_emptied(dve, f"e{t // 4}", t % 4)
                    wait_emptied(dve, f"pg{t // 4}", t % 4)
                    mult(oT[:, t, :], sg[:, t % 2, :], eT[:, t, :]).then_inc(y_ready, 1)
                if t >= 1:
                    add_sq(3, t - 1)
            rms(3, False)
            dve.wait_ge(rb_ready, 3)
            residual(2, "ple", 4, "mix")
            rms(4, True)

            dve.wait_ge(small_landed, 48)
            link(dve.tensor_scalar(snk[:, 1, :], snk[:, 0, :], -1.0, None, ALU.mult))
            rp2 = pT2[:, :, 0:256]
            for b in range(NB):
                wait_emptied(dve, "sq", b)
                rope_block(tm2[:, b, :].rearrange("p (h d) -> p h d", h=H), b, H, 32, "2", rp2)
            for b in range(NB):
                wait_emptied(dve, "skv", b)
                rope_block(skv[:, b, 0:2 * DH].rearrange("p (h d) -> p h d", h=2), b, 2, 32, "2", rp2)
            for kv in range(2):
                for c in range(2):
                    ins = dve.tensor_copy(kd2[:, :, kv, c * DH:(c + 1) * DH], skv[:, :, kv * DH:(kv + 1) * DH])
            ins.then_inc(kd_ready, 1)
            for j in range(NB):
                evac("t.sq", j, sqT[:, j, :])
            for j in range(2):
                evac("t.sk", j, skT[:, j, :])
            softmax("swa", sp2, pT2, oA, lambda b, h: tab("band")[:, P:2 * P] if b == 0 else tab("band"))
            for n, (t, w) in enumerate(((ql, QR), (kvl, KVR))):
                dve.wait_ge(ql_r, n + 1)
                link(dve.reciprocal(qs[:, n, 4:8], qs[:, n, 4:8]))
                for b in range(NB):
                    dve.tensor_scalar(t[:, b, 0:w], t[:, b, 0:w], qs[:, n, 4 + b:5 + b], None,
                                      ALU.mult).then_inc(ql_scaled, 1)
            rope_blocks(kvl[:, :, KVR:KVR + MR].rearrange("p b (h d) -> p b h d", h=1), 1, 16, "3", sp2[:, 0:2, 0:256])
            for stage, tiles, hi, lo, g, base in (("t.cq", 3, cqH, cqL, "q", 0), ("t.ck", 2, ckH, ckL, "kv", 3)):
                for j in range(tiles):
                    dve.wait_ge(c_hi_ready, base + j + 1)
                    empties(dve.scalar_tensor_tensor(
                        out=lo[:, j, :], in0=bank_of(stage, j)[:], scalar=gv[:, GV[g] + j:GV[g] + j + 1],
                        in1=hi[:, j, :].bitcast(F32), op0=ALU.mult, op1=ALU.subtract), stage, j)
            ql4 = ql[:, :, :].rearrange("p b (h d) -> p b h d", h=4)
            for i in range(2):
                for b in range(NB):
                    wait_emptied(dve, f"uq{i}", b)
                rope_blocks(ql4[:, :, :, DH:MQK], 4, 16, "3", sp2[:, 0:2, 0:256])
                for j in range(4):
                    evac(f"t.mq{i}", j, mqT[0:MQK, 4 * i + j, :], src=bank_of(f"t.mq{i}", j)[0:MQK, :])
            for i in range(2):
                if i == 0:
                    wait_filled(dve, "uq1", NB - 1)
                else:
                    wait_filled(dve, "t.mk0", 3)
                for b in range(NB):
                    kr = kvl[:, b, KVR:KVR + MR].rearrange("p (o d) -> p o d", o=1).broadcast_to([P, 4, MR])
                    ins = dve.tensor_copy(mk[:, b, :, DH:MQK], kr)
                ins.then_inc(kd_ready, 1)
                for j in range(4):
                    evac(f"t.mk{i}", j, mkT[0:MQK, 4 * i + j, :], src=bank_of(f"t.mk{i}", j)[0:MQK, :])
            softmax("mla", sp2, pT2, oB, lambda b, h: tab("causal")[:, (3 - b) * P:4 * P])
            for i in range(8):
                dve.wait_ge(u_hi_ready, 16 + i + 1)
                empties(dve.tensor_tensor(out=uL2[:, i, :], in0=bank_of("t.v", i)[:], in1=uH2[:, i, :].bitcast(F32),
                                          op=ALU.subtract), "t.v", i)
            mix(("za", "zb", "n"), (yA2, yB2), uH2, uL2, sg2, 8)
            for j in range(9):
                if j < 8:
                    wait_filled(dve, f"wp{j // 4}", j % 4)
                    empties(dve.tensor_tensor(out=xT[:, j, :], in0=bank_of(f"wp{j // 4}", j % 4)[:], in1=xT[:, j, :],
                                              op=ALU.add), f"wp{j // 4}", j % 4)
                if j >= 1:
                    low_x(3, j - 1, "ffn")
                    add_sq(5, j - 1)
            rms(5, False)
            dve.wait_ge(rb_ready, 5)
            for f in range(DFF // 256):
                if f:
                    dve.wait_ge(ff_lo, 2 * f)
                for j in range(2):
                    wait_filled(dve, f"f{f}", j)
                    empties(mult(fg[:, j, :], bank_of(f"f{f}", j)[:], rB[:]), f"f{f}", j)
                for j in range(2):
                    wait_filled(dve, f"f{f}", 2 + j)
                    empties(mult(fu[:, j, :], bank_of(f"f{f}", 2 + j)[:], rB[:]), f"f{f}", 2 + j)
                    wait_emptied(dve, f"f{f}", 2 + j)
                    dve.wait_ge(ff_act, 2 * f + j + 1)
                    mult(fg[:, j, :], fg[:, j, :], fu[:, j, :]).then_inc(ff_prod, 1)
                for j in range(2):
                    t = 2 * f + j
                    dve.wait_ge(ff_hi, t + 1)
                    dve.tensor_tensor(out=fL[:, t, :], in0=fg[:, j, :], in1=fH[:, t, :].bitcast(F32),
                                      op=ALU.subtract).then_inc(ff_lo, 1)
            for i in range(1, 8, 2):
                if i == 1:
                    wait_filled(dve, "xr", 7)
                evac("xr", i, xr[:, i // 2, 512 * (i % 2):512 * (i % 2) + 512])
            dve.wait_ge(small_landed, 64)
            for b in range(NB):
                for half in range(2):
                    i = 2 * b + half
                    part = xr[:, b, 512 * half:512 * half + 512]
                    wait_emptied(dve, "xr", i)
                    wait_filled(dve, "down", i)
                    ins = dve.tensor_tensor(out=part, in0=bank_of("down", i)[:], in1=part, op=ALU.add)
                ins.then_inc(fin_sq, 1)
                dve.wait_ge(act_step, 3 + 2 * b)
                link(dve.reciprocal(qs[:, 1, 4 + b:5 + b], qs[:, 1, b:b + 1]))
                dve.scalar_tensor_tensor(out=xr[:, b, :], in0=xr[:, b, :], scalar=qs[:, 1, 4 + b:5 + b], in1=gfin[:],
                                         op0=ALU.mult, op1=ALU.mult).then_inc(fin_ready, 1)

        @block.tensor
        def _(pe):
            def open_bank(stage, i):
                b, n = USE[stage][i]
                if n:
                    pe.wait_ge(emptied[b], n)
                return bank[b]

            def fills(ins, stage, i):
                ins.then_inc(filled[USE[stage][i][0]], 1)

            def gemm(unit, in_hi, in_lo, token_major, in_ready=None, between=None, k_first=0):
                first, n_chunks, per, n = UNITS[unit]
                total = n_chunks * per
                for c in range(first, first + n_chunks):
                    pe.wait_ge(w_hi_ready, c + 1)
                    pe.wait_ge(w_lo_ready, c + 1)
                    wh, wl = w_view(w_hi, c), w_view(w_lo, c)
                    for j in range(4):
                        if c == first:
                            out_b = open_bank(unit, j)
                        out_b = bank_of(unit, j)
                        for k in range(per):
                            kk = (c - first) * per + k
                            if in_ready and j == 0:
                                in_ready(kk)
                            ah, al = in_hi[:, k_first + kk, :], in_lo[:, k_first + kk, :]
                            if token_major:
                                tok = slice(j * P, (j + 1) * P)
                                o = out_b[:, 0:n]
                                pairs = ((ah[:, tok], wh[:, k, :]), (ah[:, tok], wl[:, k, :]), (al[:, tok], wh[:, k, :]))
                            else:
                                col = slice(j * P, (j + 1) * P)
                                o = out_b[:, :]
                                pairs = ((wh[:, k, col], ah), (wh[:, k, col], al), (wl[:, k, col], ah))
                            for m, (l, r) in enumerate(pairs):
                                ins = pe.matmul(o, l, r, start=(kk == 0 and m == 0), stop=(kk == total - 1 and m == 2))
                        if c == first + n_chunks - 1:
                            fills(ins, unit, j)
                    if c != first + n_chunks - 1:
                        ins.then_inc(w_used, 1)
                    if between and c == first:
                        between()

            def norm(n, tm_too):
                pe.wait_ge(sum_ready, 8 * n)
                o = open_bank(f"norm{n}", 0)
                fills(pe.matmul(o[:], ones[:], ssum[:], start=True, stop=True), f"norm{n}", 0)
                if tm_too:
                    o = open_bank(f"norm{n}", 1)
                    for b in range(NB):
                        ins = pe.matmul(o[:, b:b + 1], ssum[:, b * P:(b + 1) * P], ones[:, 0:1], start=True, stop=True)
                    fills(ins, f"norm{n}", 1)

            def turn_tile(stage, i, src, rows=P):
                o = open_bank(stage, i)
                for b in range(NB):
                    ins = pe.transpose(o[0:rows, b * P:(b + 1) * P], src(b), ident[:])
                fills(ins, stage, i)

            def attention(name, q, k, v, pt):
                a = ATT[name]
                for i in range(NU + 3):
                    if i < NU:
                        b, h = a.units[i]
                        k0, k1 = a.keys(b)
                        o = open_bank(name + ".l", i)
                        ins = pe.matmul(o[:, 0:(k1 - k0) * P], q(h)[:, b * P:(b + 1) * P], k(h)[:, k0 * P:k1 * P],
                                        start=True, stop=True)
                        if name == "fox":
                            ins = pe.matmul(o[:, b * P:(b + 1) * P], ident16[:], diag16[:], start=False, stop=True,
                                            skip_group_check=True)
                        fills(ins, name + ".l", i)
                    if 2 <= i < NU + 2:
                        u = i - 2
                        b, h = a.units[u]
                        k0, k1 = a.keys(b)
                        pe.wait_ge(exped, a.index * NU + u + 1)
                        o = open_bank(name + ".t", u)
                        for kb in range(k1 - k0):
                            ins = pe.transpose(o[:, kb * P:(kb + 1) * P], q_sp(name)[:, u % 3, kb * P:(kb + 1) * P], ident[:])
                        fills(ins, name + ".t", u)
                    if i >= 3:
                        u = i - 3
                        b, h = a.units[u]
                        k0, k1 = a.keys(b)
                        wait_emptied(pe, name + ".t", u)
                        if h == 0:
                            open_bank(name + ".o", b)
                        o = bank_of(name + ".o", b)[:, h * DH:(h + 1) * DH]
                        for kb in range(k0, k1):
                            ins = pe.matmul(o, pt[:, u % 2, (kb - k0) * P:(kb - k0 + 1) * P], v(kb, h),
                                            start=(kb == k0), stop=(kb == k1 - 1))
                        if h == H - 1:
                            fills(ins, name + ".o", b)
                        else:
                            ins.then_inc(pv_done, 1)

            def q_sp(name):
                return sp if ATT[name].index < 2 else sp2

            def pair(t):
                return lambda h: t[DH * (h % 2):DH * (h % 2) + DH, h // 2, :]

            def both(t):
                return lambda h: t[DH * (h % 2):DH * (h % 2) + DH, :]

            def a_ready(n):
                def wait(kk):
                    pe.wait_ge(a_hi_ready, 8 * n + kk + 1)
                    pe.wait_ge(a_lo_ready, 8 * n + kk + 1)
                return wait

            def u_from(stage, n):
                def wait(kk):
                    if stage:
                        wait_emptied(pe, stage, n + kk)
                    else:
                        pe.wait_ge(u_lo_ready, n + kk + 1)
                return wait

            pe.wait_ge(ones_ready, 1)
            pe.wait_ge(cst_landed, 32)
            pe.wait_ge(half_ready, 1)
            gemm("qi", aH, aL, True, a_ready(0), lambda: norm(1, True))
            gemm("sm", aH, aL, True)
            gemm("qa", aH, aL, True)
            pe.wait_ge(roped, 1)
            for j in range(NB):
                turn_tile("t.qi", j, lambda b: tm[:, b, j * P:(j + 1) * P])
            pe.wait_ge(kd_ready, 2)
            turn_tile("t.ki", 0, lambda b: kd[:, 0, b, :, :].rearrange("p c d -> p (c d)"))
            wait_emptied(pe, "t.qi", NB - 1)
            wait_emptied(pe, "t.ki", 0)
            for i in range(24):
                h, b = i // 3, 1 + i % 3
                o = open_bank("idx", i)
                rows = slice(DH * (h % 2), DH * (h % 2) + DH)
                fills(pe.matmul(o[:, 0:(b + 1) * P], qiT[rows, h // 2, b * P:(b + 1) * P], kdT(0)[rows, 0:(b + 1) * P],
                                start=True, stop=True), "idx", i)
            pe.wait_ge(roped, 4)
            for j in range(NB):
                turn_tile("t.qa", j, lambda b: tm[:, b, j * P:(j + 1) * P])
            turn_tile("t.ka", 0, lambda b: kd[:, 1, b, :, :].rearrange("p c d -> p (c d)"))
            pe.wait_ge(logf_ready, 1)
            o = open_bank("cum", 0)
            for jb in range(NB):
                ins = pe.matmul(o[0:H, :], lf[:, 3, jb * H:(jb + 1) * H], tab("cum")[:, (3 - jb) * P:(3 - jb) * P + S],
                                start=(jb == 0), stop=(jb == NB - 1))
            fills(ins, "cum", 0)
            gemm("qb", aH, aL, False)
            gemm("kb", aH, aL, False)
            gemm("vb", aH, aL, True)
            for b in range(NB):
                wait_emptied(pe, "vb", b)
            pe.wait_ge(qb_scaled, 8)
            attention("fox", pair(qbT), pair(kbT), lambda kb, h: vb[:, kb, h * DH:(h + 1) * DH], pT)
            attention("dsa", pair(qaT), both(kdT(1)), lambda kb, h: sm[:, kb, SM_VA:SM_VA + DH], pT)
            gemm("ga", aH, aL, False)
            gemm("gb", aH, aL, False)
            for i in range(8):
                wait_emptied(pe, "dsa.o" if i < 4 else "fox.o", NB - 1)
                att, j = ((qiT, tm)[i // 4], i % 4)
                turn_tile("t.u", i, lambda b: att[:, b, j * P:(j + 1) * P])
            for n, u in enumerate(("ya0", "ya1", "yb0", "yb1")):
                gemm(u, uH, uL, False, u_from(None, 4 * (n // 2)), k_first=4 * (n // 2))
            for n in range(4):
                gemm(f"m{n}", aH, aL, False)
            for n in range(2):
                gemm(f"wo{n}", uH, uL, False, u_from(None, 8))
            pe.wait_ge(p_lo_ready, 2)
            gemm("e0", pH, pL, False)
            norm(2, False)
            gemm("e1", pH, pL, False)
            gemm("pg0", aH, aL, False, a_ready(1))
            gemm("pg1", aH, aL, False)
            norm(3, False)
            gemm("sq", aH, aL, True, a_ready(2), lambda: norm(4, True))
            gemm("skv", aH, aL, True)
            pe.wait_ge(roped, 4 + NB)
            for j in range(NB):
                turn_tile("t.sq", j, lambda b: tm2[:, b, j * P:(j + 1) * P])
            pe.wait_ge(kd_ready, 3)
            for kv in range(2):
                turn_tile("t.sk", kv, lambda b: kd2[:, b, kv, :])
            for j in range(NB):
                wait_emptied(pe, "t.sq", j)
            for j in range(2):
                wait_emptied(pe, "t.sk", j)
            attention("swa", pair(sqT), lambda h: skT[DH * (h % 2):DH * (h % 2) + DH, h // 4, :],
                      lambda kb, h: skv[:, kb, 2 * DH + DH * (h // 4):2 * DH + DH * (h // 4) + DH], pT2)
            gemm("ql", aH, aL, True)
            gemm("kvl", aH, aL, True)
            pe.wait_ge(ql_scaled, 4)
            for j in range(3):
                turn_tile("t.cq", j, lambda b: ql[:, b, j * P:(j + 1) * P])
            pe.wait_ge(ql_scaled, 8)
            for j in range(2):
                turn_tile("t.ck", j, lambda b: kvl[:, b, j * P:(j + 1) * P])
            for i in range(2):
                gemm(f"uq{i}", cqH, cqL, True, u_from("t.cq", 0))
                pe.wait_ge(roped, 6 + 2 * NB + i)
                for j in range(4):
                    turn_tile(f"t.mq{i}", j, lambda b: ql[:, b, j * MQK:(j + 1) * MQK], rows=MQK)
            for i in range(2):
                gemm(f"ukv{i}", ckH, ckL, True, u_from("t.ck", 0))
                pe.wait_ge(kd_ready, 4 + i)
                pe.wait_ge(mk_ready, 4 * i + 4)
                for j in range(4):
                    turn_tile(f"t.mk{i}", j, lambda b: mk[:, b, j, :], rows=MQK)
            for b in range(NB):
                wait_emptied(pe, "ukv1", b)
            for j in range(4):
                wait_emptied(pe, "t.mk1", j)
            attention("mla", lambda h: mqT[0:MQK, h, :], lambda h: mkT[0:MQK, h, :],
                      lambda kb, h: mv[:, kb, h, :], pT2)
            for i in range(8):
                wait_emptied(pe, "swa.o" if i < 4 else "mla.o", NB - 1)
                att, j = ((oA, oB)[i // 4], i % 4)
                turn_tile("t.v", i, lambda b: att[:, b, j * P:(j + 1) * P])
            for n, u in enumerate(("za0", "za1", "zb0", "zb1")):
                gemm(u, uH2, uL2, False, u_from("t.v", 4 * (n // 2)), k_first=4 * (n // 2))
            for n in range(4):
                gemm(f"n{n}", aH, aL, False)
            for n in range(2):
                gemm(f"wp{n}", uH2, uL2, False, u_from(None, 16))
            gemm("f0", aH, aL, False, a_ready(3), lambda: norm(5, False))
            for f in range(1, DFF // 256):
                gemm(f"f{f}", aH, aL, False)
            for i in range(8):
                b, half = i // 2, i % 2
                o = open_bank("xr", i)
                for j in range(4):
                    ins = pe.transpose(o[:, j * P:(j + 1) * P], xT[:, 4 * half + j, b * P:(b + 1) * P], ident[:])
                fills(ins, "xr", i)
            first, n_chunks, per, _ = UNITS["down"]
            for c in range(first, first + n_chunks):
                pe.wait_ge(w_hi_ready, c + 1)
                pe.wait_ge(w_lo_ready, c + 1)
                wh, wl = w_view(w_hi, c), w_view(w_lo, c)
                pe.wait_ge(ff_lo, min(2 * (c - first) + 2, NF))
                for i in range(8):
                    b, half = i // 2, i % 2
                    if c == first:
                        open_bank("down", i)
                    tok, col = slice(b * P, (b + 1) * P), slice(512 * half, 512 * half + 512)
                    for k in range(per):
                        kk = (c - first) * per + k
                        for m, (l, r) in enumerate(((fH, wh), (fH, wl), (fL, wh))):
                            ins = pe.matmul(bank_of("down", i)[:], l[:, kk, tok], r[:, k, col],
                                            start=(kk == 0 and m == 0), stop=(kk == NF - 1 and m == 2))
                    if c == first + n_chunks - 1:
                        fills(ins, "down", i)
                if c != first + n_chunks - 1:
                    ins.then_inc(w_used, 1)


NAMES = ["w_in", "w_branch_a", "w_branch_b", "w_merge", "w_out", "w_ple", "w_ple_gate", "b_forget",
         "w_in_2", "swa_sinks_2", "w_uq_2", "w_ukv_2", "w_o_swa_2", "w_o_mla_2", "w_out_2", "w_gate_2",
         "w_up_2", "w_down_2"]


def kernel(**inputs):
    import concourse.bacc as bacc
    from concourse.bass_utils import run_bass_kernel_spmd

    order = ["g_pre", "g_post", "g_ple", "mix_norm_g_2", "ffn_norm_g_2", "q_norm_g_2", "kv_norm_g_2"]
    arrays = {n: np.ascontiguousarray(inputs[n]) for n in NAMES}
    arrays["gains"] = np.ascontiguousarray(
        np.concatenate([np.asarray(inputs[n]).reshape(-1, P).T for n in order], axis=1))
    arrays["final_norm_g_2"] = np.ascontiguousarray(np.asarray(inputs["final_norm_g_2"]).reshape(1, D))
    arrays["xT"] = np.ascontiguousarray(np.asarray(inputs["x"])[0].T)
    arrays["pT"] = np.ascontiguousarray(np.asarray(inputs["p"])[0, 0].T)
    arrays["cst"] = constants()
    nc = bacc.Bacc("TRN2", target_bir_lowering=False, num_devices=1)
    dram = {n: nc.dram_tensor(f"in_{n}", a.shape, mybir.dt.from_np(a.dtype), kind="ExternalInput").ap()
            for n, a in arrays.items()}
    out = nc.dram_tensor("out_x", (1, S, D), F32, kind="ExternalOutput").ap()
    build(nc, dram, out)
    r = run_bass_kernel_spmd(nc, [{f"in_{n}": a for n, a in arrays.items()}], core_ids=[0])
    return r.results[0]["out_x"]
```

```python
from contextlib import ExitStack

import numpy as np

import concourse.bass as bass
from concourse import mybir

F32 = mybir.dt.float32
F32R = mybir.dt.float32r
BF16 = mybir.dt.bfloat16
ALU = mybir.AluOpType
ACT = mybir.ActivationFunctionType

P = 128
S = 512
NB = S // P
D = 1024
KD = D // P
DH = 64
H = 8
WA = H * DH
TOPK = min(256, S // 4)
EPS = 1e-6
NEG = -1e30
TAKEN = -3e38
D_PLE = 256
QR, KVR, MR = 384, 256, 32
MQK = DH + MR
DFF = 2816
CH = 2048

O_QA, O_KA, O_GA, O_QI, O_KI = 0, 512, 640, 1152, 1664
O_QB, O_KB, O_VB, O_FB, O_GB = 1736, 2248, 2760, 3272, 3280
O2_Q, O2_KV, O2_QL, O2_KVL, O2_GA, O2_GB = 0, 512, 768, 1152, 1440, 2464
SM_W = 208
SM_KI, SM_WI, SM_FB, SM_KA, SM_VA = 0, 64, 72, 80, 144

_C = {}
_at = 0
for _n, _w in (("ident", P), ("cum", 3 * P + S), ("cos1", NB * 8), ("sin1", NB * 8), ("cos2", NB * 32),
               ("sin2", NB * 32), ("cos3", NB * 16), ("sin3", NB * 16), ("band", 2 * P), ("causal", 3 * P + P)):
    _C[_n] = (_at, _w)
    _at += _w
CST_W = _at
GV = {"pre": 0, "post": 8, "ple": 16, "mix": 24, "ffn": 32, "q": 40, "kv": 43}
GV_W = 45


def constants():
    f = np.float32
    c = np.zeros((P, CST_W), f)
    q = np.arange(P)[:, None]

    def put(name, a):
        o, w = _C[name]
        c[:, o:o + w] = a

    put("ident", np.eye(P, dtype=f))
    k = np.arange(4 * P)[None, :] - 3 * P
    put("causal", np.where(k <= q, 0, NEG).astype(f))
    k = np.arange(3 * P + S)[None, :] - 3 * P
    put("cum", np.where(k >= q, 1, 0).astype(f))
    kj = np.arange(2 * P)[None, :]
    diff = q - kj + P
    put("band", np.where((diff >= 0) & (diff < P), 0, NEG).astype(f))
    pos = (np.arange(NB)[None, :, None] * P + np.arange(P)[:, None, None]).astype(f)
    for n, half, freqs in (
        ("1", 8, f(500000.0) ** (-np.arange(8, dtype=f) / f(8))),
        ("2", 32, f(10000.0) ** (-np.arange(0, 64, 2, dtype=f) / f(64))),
        ("3", 16, f(10000.0) ** (-np.arange(0, 32, 2, dtype=f) / f(32))),
    ):
        ang = (pos * freqs.astype(f)[None, None, :]).astype(f)
        put("cos" + n, np.cos(ang).reshape(P, NB * half))
        put("sin" + n, np.sin(ang).reshape(P, NB * half))
    return c


def plan_weights():
    chunks, units = [], {}

    def unit(name, rows, per, pieces):
        first, n = len(chunks), sum(w for _, _, w in pieces)
        sizes = per if isinstance(per, list) else [per] * (rows // P // per)
        k = 0
        for size in sizes:
            off, ps = 0, []
            for arr, col, w in pieces:
                ps.append((arr, k * P, col, w, off))
                off += w
            assert size * n <= CH
            chunks.append((size, n, ps, k))
            k += size
        units[name] = (first, len(sizes), rows // P, n)

    w1, w2 = "w_in", "w_in_2"
    unit("qi", D, [1, 1, 2, 4], [(w1, O_QI, WA)])
    unit("sm", D, 8, [(w1, O_KI, 72), (w1, O_FB, 8), (w1, O_KA, 128)])
    unit("qb", D, 4, [(w1, O_QB, WA)])
    unit("kb", D, 4, [(w1, O_KB, WA)])
    unit("vb", D, 4, [(w1, O_VB, WA)])
    unit("qa", D, 4, [(w1, O_QA, WA)])
    unit("ga", D, 4, [(w1, O_GA, WA)])
    unit("gb", D, 4, [(w1, O_GB, WA)])
    for n, arr in (("ya", "w_branch_a"), ("yb", "w_branch_b")):
        for i in range(2):
            unit(f"{n}{i}", WA, 4, [(arr, 512 * i, 512)])
    for i in range(4):
        unit(f"m{i}", D, 4, [("w_merge", 512 * i, 512)])
    for i in range(2):
        unit(f"wo{i}", D, 4, [("w_out", 512 * i, 512)])
    for i in range(2):
        unit(f"e{i}", D_PLE, 2, [("w_ple", 512 * i, 512)])
    for i in range(2):
        unit(f"pg{i}", D, 4, [("w_ple_gate", 512 * i, 512)])
    unit("sq", D, 4, [(w2, O2_Q, 512)])
    unit("skv", D, 8, [(w2, O2_KV, 256)])
    unit("ql", D, 4, [(w2, O2_QL, QR)])
    unit("kvl", D, 4, [(w2, O2_KVL, KVR + MR)])
    for i in range(2):
        unit(f"uq{i}", QR, 3, [("w_uq_2", 384 * i, 384)])
        unit(f"ukv{i}", KVR, 2, [("w_ukv_2", 512 * i, 512)])
    for n, arr in (("za", "w_o_swa_2"), ("zb", "w_o_mla_2")):
        for i in range(2):
            unit(f"{n}{i}", WA, 4, [(arr, 512 * i, 512)])
    for i in range(4):
        unit(f"n{i}", D, 4, [(w2, O2_GA + 512 * i, 512)])
    for i in range(2):
        unit(f"wp{i}", D, 4, [("w_out_2", 512 * i, 512)])
    for i in range(DFF // 256):
        unit(f"f{i}", D, 4, [("w_gate_2", 256 * i, 256), ("w_up_2", 256 * i, 256)])
    unit("down", DFF, 2, [("w_down_2", 0, D)])
    return chunks, units


CHUNKS, UNITS = plan_weights()
LAST_OF = {f + n - 1: name for name, (f, n, _, _) in UNITS.items()}


class Attn:

    def __init__(self, name, index, keys):
        self.name, self.index = name, index
        self.units = [(h, b) for h in range(H) for b in range(NB)]
        self.keys = keys

    def queries(self, kb):
        seen = [b for b in range(NB) if self.keys(b)[0] <= kb < self.keys(b)[1]]
        return seen[0], seen[-1] + 1


def causal_keys(b):
    return 0, b + 1


def band_keys(b):
    return max(b - 1, 0), b + 1


ATT = {n: Attn(n, i, k) for i, (n, k) in enumerate((("fox", causal_keys), ("dsa", causal_keys),
                                                    ("swa", band_keys), ("mla", causal_keys)))}
NU = NB * H
PAIR_HI_AT, PAIR_LO_AT = {1: 1, 5: 2, 13: 3}, {0: 1, 3: 2, 11: 3}
ROUNDS_FIRST = 10
PT_W = NB * (NB + 1)
RING = 5
LAG_R, LAG_T, LAG_HI, LAG_LO, LAG_PV = 2, 4, 4, 5, 8


def plan_banks():
    count = [0] * 8
    use = {}

    def fill(stage, banks):
        use[stage] = []
        for b in banks:
            use[stage].append((b, count[b]))
            count[b] += 1

    four = [0, 1, 2, 3]

    def attention(name):
        a = ATT[name]
        use[name + ".l"], use[name + ".t"], use[name + ".o"] = [], [], []
        for i in range(NU):
            for stage, b in ((".l", (4, 5, 2)[i % 3]), (".t", (6, 7, 3)[i % 3])):
                use[name + stage].append((b, count[b]))
                count[b] += 1
        for h in range(H):
            use[name + ".o"].append((h % 2, count[h % 2]))
            count[h % 2] += 1

    fill("qi", four); fill("norm1", [6, 7]); fill("sm", four)
    fill("qb", four)
    fill("t.qi", [4, 5, 6, 7] * 2); fill("t.ki", [4, 5])
    fill("idx", [4 + i % 4 for i in range(24)])
    fill("t.ka", [4, 5]); fill("cum", [6])
    fill("kb", four); fill("vb", four)
    attention("fox")
    fill("qa", four); fill("ga", four); fill("gb", four)
    fill("t.qa", [4, 5, 6, 7] * 2)
    attention("dsa")
    for n in ("ya0", "ya1", "yb0", "yb1", "m0", "m1", "m2", "m3", "wo0", "wo1", "e0"):
        fill(n, four)
    fill("norm2", [6, 7]); fill("e1", four); fill("pg0", four); fill("pg1", four)
    fill("norm3", [6, 7])
    fill("sq", four); fill("norm4", [6, 7]); fill("skv", four)
    fill("ql", four); fill("kvl", four)
    fill("t.sq", [4, 5, 6, 7] * 2); fill("t.sk", [4, 5, 6, 7])
    fill("t.cq", [4, 5, 6]); fill("t.ck", [7, 4])
    attention("swa")
    fill("uq0", four); fill("ukv0", four); fill("t.mq0", [4, 5, 6, 7])
    fill("uq1", four); fill("t.mk0", [4, 5, 6, 7])
    fill("ukv1", four); fill("t.mq1", [4, 5, 6, 7]); fill("t.mk1", [4, 5, 6, 7])
    attention("mla")
    for n in ("za0", "za1", "zb0", "zb1", "n0", "n1", "n2", "n3", "wp0", "wp1"):
        fill(n, four)
    fill("f0", four); fill("norm5", [6, 7])
    for i in range(1, DFF // 256):
        fill(f"f{i}", four)
    fill("xr", list(range(8))); fill("down", list(range(8)))
    return use


USE = plan_banks()


def build(nc, dram, out):
    ctx = ExitStack()
    with ctx:
        def sb(name, shape, dt=F32):
            return ctx.enter_context(nc.sbuf_tensor(name, shape, dt))

        def sem(name):
            return ctx.enter_context(nc.semaphore(name))

        def place(name, offset, shape, dt=F32):
            with ExitStack() as st:
                if offset:
                    st.enter_context(nc.sbuf_tensor("below_" + name, [P, int(offset * 256)], F32))
                return st.enter_context(nc.sbuf_tensor(name, shape, dt))

        w_raw = sb("w_raw", [P, 2, CH])
        w_hi = sb("w_hi", [P, 2, CH], F32R)
        w_lo = sb("w_lo", [P, 2, CH], F32R)
        aH = sb("aH", [P, KD, S], F32R)
        aL = sb("aL", [P, KD, S], F32R)
        rB = sb("rB", [P, S])
        ssum = sb("ssum", [P, S])
        sq = sb("sq", [P, 2, S])
        rT = sb("rT", [P, NB])
        ident = sb("ident", [P, P])
        ident16 = sb("ident16", [P, P], BF16)
        diag16 = sb("diag16", [P, P], BF16)
        ones = sb("ones", [P, P])
        gv = sb("gv", [P, GV_W])
        mx = sb("mx", [P, NU])
        nbias = sb("nbias", [P, NU])
        sums = sb("sums", [P, NU])
        rsum = sb("rsum", [P, NU])
        m8 = sb("m8", [P, 3, 8])
        snk = sb("snk", [P, 2, H])
        bfg = sb("bfg", [P, H])
        lf = sb("lf", [P, 4, NB * H])
        qs = sb("qs", [P, 2, H])

        cst = place("cst", 106.5, [P, CST_W - P])
        xT = place("xT", 0, [P, KD, S])
        tmI = place("tmI", 16, [P, NB, S])
        spI = place("spI", 24, [P, NB, H, P], F32R)
        qiS = place("qiS", 40, [P, H, S], F32R)
        kiS = place("kiS", 56, [P, 2, S], F32R)
        kdI = place("kdI", 60, [P, 2, NB, P], F32R)
        kaS = place("kaS", 64, [P, 2, S], F32R)
        vaS = place("vaS", 68, [P, 2, NB, P], F32R)
        sm = place("sm", 94, [P, NB, SM_W])
        rp = place("rp", 104, [P, 2, 256])
        sc = place("sc", 72, [P, 9 * P])
        sp = place("sp", 78, [P, RING, S])
        attB = place("attB", 90, [P, NB, S])
        attA = place("attA", 98, [P, NB, S])
        cT = place("cT", 102, [H, S])
        qbT, kbT = place("qbT", 0, [P, NB, S]), place("kbT", 8, [P, NB, S])
        fQ, fK = place("fQ", 16, [P, 2, S], F32R), place("fK", 20, [P, 2, 2, S], F32R)
        tQ, tK = place("tQ", 102, [P, S]), place("tK", 104, [P, S])
        vbS = place("vbS", 28, [P, 2, NB, S], F32R)
        pT = place("pT", 44, [P, 2, PT_W, P], F32R)
        cB = place("cB", 98, [P, 2, S])
        tmA = place("tmA", 0, [P, NB, S])
        qaS = place("qaS", 8, [P, H, S], F32R)
        gA, gB = place("gA", 24, [P, NB, S]), place("gB", 32, [P, NB, S])
        spA = place("spA", 44, [P, NB, H, P], F32R)
        sg, tmp = place("sg", 16, [P, 2, S]), place("tmp", 20, [P, 2, S])
        pH, pL = place("pH", 24, [P, 2, S], F32R), place("pL", 28, [P, 2, S], F32R)
        pr = place("pr", 32, [P, 2, S])
        uH, uL = place("uH", 40, [P, KD, S], F32R), place("uL", 56, [P, KD, S], F32R)
        yA, yB = place("yA", 72, [P, KD, S]), place("yB", 88, [P, KD, S])
        pT2 = place("pT2", 0, [P, 2, PT_W, P], F32R)
        tm2 = place("tm2", 16, [P, NB, S])
        sp2 = place("sp2", 24, [P, NB, H, P], F32R)
        sqS = place("sqS", 40, [P, H, S], F32R)
        skv = place("skv", 56, [P, NB, 256])
        kd2 = place("kd2", 60, [P, 2, 2, NB, P], F32R)
        skS = place("skS", 68, [P, 2, 2, S], F32R)
        vsS = place("vsS", 76, [P, 2, 2, NB, P], F32R)
        sc2 = place("sc2", 92.5, [P, RING, S])
        oA = place("oA", 102.5, [P, NB, S])
        rp2, rp3 = place("rp2", 102.5, [P, 2, 256]), place("rp3", 98.5, [P, 2, 256])
        ql = place("ql", 92.5, [P, NB, QR])
        cqH, cqL = place("cqH", 28, [P, 3, S], F32R), place("cqL", 34, [P, 3, S], F32R)
        kvl = place("kvl", 88, [P, NB, KVR + MR])
        ckH, ckL = place("ckH", 20, [P, 2, S], F32R), place("ckL", 24, [P, 2, S], F32R)
        mk = [place(f"mk{i}", 6 * i, [P, NB, 4, MQK]) for i in range(2)]
        uq = [place(f"uq{i}", 92.5 - 80.5 * i, [P, NB, QR]) for i in range(2)]
        mvS = place("mvS", 44, [P, 2, NB, H, DH], F32R)
        mqT, mkT = place("mqT", 60, [P, H, S]), place("mkT", 76, [P, H, S])
        mQ, mK = place("mQ", 28, [P, 2, 2, S], F32R), place("mK", 36, [P, 2, 2, S], F32R)
        oB = place("oB", 20, [P, NB, S])
        sg2 = place("sg2", 16, [P, 2, S])
        uH2, uL2 = place("uH2", 40, [P, KD, S], F32R), place("uL2", 56, [P, KD, S], F32R)
        yA2, yB2 = place("yA2", 72, [P, KD, S]), place("yB2", 88, [P, KD, S])
        NF = DFF // P
        fH, fL = place("fH", 16, [P, NF, S], F32R), place("fL", 60, [P, NF, S], F32R)
        fg, fu = place("fg", 104, [P, 2, S]), place("fu", 108, [P, 2, S])
        gfin = place("gfin", 112, [P, D])
        xr = xT[:, :, :].rearrange("p a b -> p (a b)").rearrange("p (b d) -> p b d", b=NB)
        oT, eT = yB, yA

        def tab(name):
            o, w = _C[name]
            return cst[:, o - P:o - P + w]

        def rope_tab(name, half):
            return tab(name).rearrange("p (b f) -> p b f", b=NB)

        bank = [ctx.enter_context(nc.psum_tensor(f"bank{i}", [P, S], F32)) for i in range(8)]
        filled = [sem(f"filled{i}") for i in range(8)]
        emptied = [sem(f"emptied{i}") for i in range(8)]

        w_landed = [sem(f"w_landed{i}") for i in range(2)]
        w_hi_ready, w_lo_ready, w_used = sem("w_hi_ready"), sem("w_lo_ready"), sem("w_used")
        x_landed = [sem(f"x_landed{i}") for i in range(4)]
        gains_landed, cst_landed, small_landed, p_landed = sem("gains_landed"), sem("cst_landed"), sem("small_landed"), sem("p_landed")
        ones_ready, half_ready = sem("ones_ready"), sem("half_ready")
        sq_ready, sum_ready, rt_ready = sem("sq_ready"), sem("sum_ready"), sem("rt_ready")
        diag_ready, gate_raw = sem("diag_ready"), sem("gate_raw")
        a_hi_ready, a_lo_ready = sem("a_hi_ready"), sem("a_lo_ready")
        roped, kr_copied = sem("roped"), sem("kr_copied")
        logf_ready, cum_stored = sem("logf_ready"), sem("cum_stored")
        cum_landed = [sem(f"cum_landed{i}") for i in range(2)]
        lf_in, lf_ln = sem("lf_in"), sem("lf_ln")
        scored, idx_done, chosen = sem("scored"), sem("idx_done"), sem("chosen")
        qb_scaled = sem("qb_scaled")
        biased, exped = sem("biased"), sem("exped")
        u_mul, u_hi_ready, u_lo_ready = sem("u_mul"), sem("u_hi_ready"), sem("u_lo_ready")
        gate_ready = sem("gate_ready")
        split_hi, split_lo, v_lo_ready = sem("split_hi"), sem("split_lo"), sem("v_lo_ready")
        row_inv, scaled, sinked, p_hi = sem("row_inv"), sem("scaled"), sem("sinked"), sem("p_hi")
        pair_hi_ready, pair_lo_ready = sem("pair_hi_ready"), sem("pair_lo_ready")
        head_landed = [sem(f"head_landed{i}") for i in range(2)]
        mla_hi_ready, mla_lo_ready = sem("mla_hi_ready"), sem("mla_lo_ready")
        x_back, x_stored = sem("x_back"), sem("x_stored")
        sg_ready, z_ready = sem("sg_ready"), sem("z_ready")
        p_hi_ready, p_lo_ready = sem("p_hi_ready"), sem("p_lo_ready")
        x_new, y_ready = sem("x_new"), sem("y_ready")
        ql_sq, ql_r, ql_scaled = sem("ql_sq"), sem("ql_r"), sem("ql_scaled")
        c_hi_ready, c_lo_ready = sem("c_hi_ready"), sem("c_lo_ready")
        mk_ready = sem("mk_ready")
        ff_act, ff_prod, ff_hi, ff_lo = sem("ff_act"), sem("ff_prod"), sem("ff_hi"), sem("ff_lo")
        fin_ready, fin_sq, fin_rms, stored = sem("fin_ready"), sem("fin_sq"), sem("fin_rms"), sem("stored")
        dve_step, act_step = sem("dve_step"), sem("act_step")

        x_dram = nc.dram_tensor("x_scratch", (P, KD * S), F32, kind="Internal").ap()
        cum_dram = nc.dram_tensor("cum_scratch", (H, S), F32, kind="Internal").ap()

        def pair_hi(part, j):
            return ((tQ, tK)[part][:, :], (qbT, kbT)[part][:, 0, :], (tQ, tK)[part][:, :], (qbT, kbT)[part][:, 1, :])[j].bitcast(F32R)

        def pair_lo(part, j):
            return (qbT, kbT)[part][:, j, :].bitcast(F32R)

        def att_done(name):
            b, n = USE[name + ".o"][H - 1]
            return emptied[b], n + 1

        def wait_filled(eng, stage, i):
            b, n = USE[stage][i]
            eng.wait_ge(filled[b], n + 1)

        def wait_emptied(eng, stage, i):
            b, n = USE[stage][i]
            eng.wait_ge(emptied[b], n + 1)

        def bank_of(stage, i):
            return bank[USE[stage][i][0]]

        def empties(ins, stage, i):
            ins.then_inc(emptied[USE[stage][i][0]], 1)

        def wait_used(eng, c):
            if c in LAST_OF:
                wait_filled(eng, LAST_OF[c], len(USE[LAST_OF[c]]) - 1)
            else:
                eng.wait_ge(w_used, sum(1 for i in range(c + 1) if i not in LAST_OF))

        def p_place(a, h, kb, b):
            if a.keys is band_keys:
                return 2 * NB * (h % 2) + kb + b
            return NB * kb + b if h % 2 == 0 else NB * NB - (NB + 1) * kb + b

        def p_order(a, h, b):
            k0, k1 = a.keys(b)
            return sorted(range(k0, k1), key=lambda kb: p_place(a, h, kb, b))

        def p_views(a, i, pt, part):
            h, b = a.units[i]
            at = [p_place(a, h, kb, b) for kb in p_order(a, h, b)]
            step = at[1] - at[0] if len(at) > 1 else 1
            return pt[:, part, at[0]:at[-1] + 1:step, :]

        def t_view(a, i):
            h, b = a.units[i]
            n = (a.keys(b)[1] - a.keys(b)[0]) * P
            return bank_of(a.name + ".t", i)[:, 0:n].rearrange("p (k q) -> p k q", q=P)

        def w_view(buf, c):
            per, n, _, _ = CHUNKS[c]
            return buf[:, c % 2, 0:per * n].rearrange("p (k n) -> p k n", n=n)

        landed, total = [], [0, 0]
        for c, (_, _, ps, _) in enumerate(CHUNKS):
            total[c % 2] += 16 * len(ps)
            landed.append(total[c % 2])

        block = ctx.enter_context(nc.Block())

        @block.sync
        def _(sp_):
            sp_.dma_start(gv[:], dram["gains"]).then_inc(gains_landed, 16)
            xv = dram["xT"].rearrange("(k p) t -> p k t", p=P)

            def load(c):
                if c >= 2:
                    sp_.wait_ge(w_hi_ready, c - 1)
                    sp_.wait_ge(w_lo_ready, c - 1)
                per, n, ps, _ = CHUNKS[c]
                v = w_view(w_raw, c)
                for arr, r0, c0, w, off in ps:
                    src = dram[arr][0, r0:r0 + per * P, c0:c0 + w].rearrange("(k p) n -> p k n", p=P)
                    sp_.dma_start(v[:, :, off:off + w], src).then_inc(w_landed[c % 2], 16)

            def load_cum(h):
                sp_.dma_start(cB[:, h % 2, :], cum_dram[h:h + 1, :].broadcast_to([P, S])).then_inc(cum_landed[h % 2], 16)

            def stack_head(h):
                sp_.wait_ge(pair_hi_ready, 2 * (h // 2) + 2)
                sp_.wait_ge(pair_lo_ready, 2 * (h // 2) + 2)
                r = slice(DH * (h % 2), DH * (h % 2) + DH)
                hi, lo = ([f(p, h // 2)[r, :] for p in range(2)] for f in (pair_hi, pair_lo))
                for dst, top, bottom in ((fQ[:, h % 2, :], hi[0], lo[0]), (fK[:, h % 2, 0, :], hi[1], hi[1]),
                                         (fK[:, h % 2, 1, :], lo[1], lo[1])):
                    sp_.dma_start(dst[0:DH].bitcast(F32), top.bitcast(F32)).then_inc(head_landed[h % 2], 16)
                    sp_.dma_start(dst[DH:P].bitcast(F32), bottom.bitcast(F32)).then_inc(head_landed[h % 2], 16)

            for i in range(4):
                sp_.dma_start(xT[:, 2 * i:2 * i + 2, :], xv[:, 2 * i:2 * i + 2, :]).then_inc(x_landed[i], 16)
                if i < 2:
                    load(i)
            sp_.dma_start(bfg[:], dram["b_forget"].broadcast_to([P, H])).then_inc(small_landed, 16)
            sp_.dma_start(snk[:, 0, :], dram["swa_sinks_2"].broadcast_to([P, H])).then_inc(small_landed, 16)
            for c in range(2, len(CHUNKS)):
                load(c)
                if c == UNITS["qi"][0] + 2:
                    sp_.dma_start(ident[:], dram["cst"][:, 0:P]).then_inc(cst_landed, 16)
                    sp_.dma_start(cst[:], dram["cst"][:, P:]).then_inc(cst_landed, 16)
                if c == UNITS["vb"][0]:
                    wait_emptied(sp_, "cum", 0)
                    sp_.dma_start(cum_dram, cT[:, :]).then_inc(cum_stored, 16)
                    sp_.wait_ge(cum_stored, 16)
                    for h in range(2):
                        load_cum(h)
                if c == UNITS["qa"][0] + 1:
                    for h in range(2):
                        stack_head(h)
                if c == UNITS["qa"][0] + 2:
                    for h in range(2, H):
                        wait_emptied(sp_, "fox.l", NB * (h - 1) - 1)
                        load_cum(h)
                        stack_head(h)
                if c == UNITS["m0"][0]:
                    wait_emptied(sp_, "dsa.o", H - 1)
                    sp_.dma_start(xT[:], xv).then_inc(x_back, 16)
                if c == UNITS["m1"][0]:
                    sp_.wait_ge(u_lo_ready, 8)
                    sp_.dma_start(pr[:], dram["pT"].rearrange("(k p) t -> p k t", p=P)).then_inc(p_landed, 16)
                if c == UNITS["skv"][0]:
                    sp_.wait_ge(x_new, 16)
                    sp_.dma_start(x_dram, xT[:].rearrange("p k t -> p (k t)")).then_inc(x_stored, 16)
                if c == UNITS["n0"][0]:
                    wait_emptied(sp_, "mla.o", H - 1)
                    sp_.dma_start(xT[:].rearrange("p k t -> p (k t)"), x_dram).then_inc(x_back, 16)
                if c == UNITS["f2"][0]:
                    sp_.dma_start(gfin[:], dram["final_norm_g_2"].broadcast_to([P, D])).then_inc(small_landed, 16)
            for b in range(NB):
                sp_.wait_ge(fin_ready, b + 1)
                sp_.dma_start(out[0, b * P:(b + 1) * P, :], xr[:, b, :]).then_inc(stored, 16)
            sp_.wait_ge(stored, 16 * NB)

        @block.gpsimd
        def _(pool):
            pool.memset(ones[:], 1.0).then_inc(ones_ready, 1)
            next_chunk = [0]

            def lo_through(c_end):
                for c in range(next_chunk[0], min(c_end + 1, len(CHUNKS))):
                    n = CHUNKS[c][0] * CHUNKS[c][1]
                    pool.wait_ge(w_hi_ready, c + 1)
                    pool.tensor_tensor(out=w_lo[:, c % 2, 0:n], in0=w_raw[:, c % 2, 0:n],
                                       in1=w_hi[:, c % 2, 0:n].bitcast(F32), op=ALU.subtract).then_inc(w_lo_ready, 1)
                    next_chunk[0] = c + 1

            for u, t in (("qb", qbT), ("kb", kbT)):
                lo_through(UNITS[u][0] + UNITS[u][1] + 1)
                wait_emptied(pool, "norm1", 1)
                for j in range(NB):
                    wait_emptied(pool, u, j)
                    pool.tensor_tensor(out=t[:, j, :], in0=t[:, j, :], in1=rB[:], op=ALU.mult).then_inc(qb_scaled, 1)

            def scale_rows(name, sc_):
                a = ATT[name]
                for i in range(NU):
                    h, b = a.units[i]
                    n = (a.keys(b)[1] - a.keys(b)[0]) * P
                    pool.wait_ge(row_inv, a.index * NU + i + 1)
                    s = sc_[:, i % RING, 0:n]
                    pool.tensor_scalar(s, s, rsum[:, i:i + 1], 1.0, ALU.mult, ALU.mult).then_inc(scaled, 1)
                    if name == "fox" and i in PAIR_LO_AT:
                        split_pair(PAIR_LO_AT[i])
                    if name == "mla" and b == NB - 1 and h + 2 < H:
                        pool.wait_ge(scaled, a.index * NU + i + 1)
                        split_head(h + 2)

            def split_pair(j):
                for p, t in enumerate((qbT, kbT)):
                    pool.wait_ge(pair_hi_ready, 2 * j + p + 1)
                    pool.tensor_tensor(out=pair_lo(p, j), in0=t[:, j, :], in1=pair_hi(p, j).bitcast(F32),
                                       op=ALU.subtract).then_inc(pair_lo_ready, 1)

            def split_head(h):
                for p, (t, m_) in enumerate(((mqT, mQ), (mkT, mK))):
                    pool.wait_ge(mla_hi_ready, 2 * h + p + 1)
                    pool.tensor_tensor(out=m_[0:MQK, h % 2, 1, :], in0=t[0:MQK, h, :],
                                       in1=m_[0:MQK, h % 2, 0, :].bitcast(F32), op=ALU.subtract).then_inc(mla_lo_ready, 1)
                pool.wait_ge(mla_lo_ready, 2 * h + 2)

            lo_through(UNITS["vb"][0] + UNITS["vb"][1] - 1)
            pool.wait_ge(qb_scaled, 8)
            split_pair(0)
            lo_through(UNITS["vb"][0] + UNITS["vb"][1])
            scale_rows("fox", sp)
            for u, t in (("ga", gA), ("gb", gB)):
                lo_through(UNITS[u][0] + UNITS[u][1] + (1 if u == "ga" else -1))
                for j in range(NB):
                    wait_emptied(pool, u, j)
                    pool.tensor_tensor(out=t[:, j, :], in0=t[:, j, :], in1=rB[:], op=ALU.mult).then_inc(gate_raw, 1)
            lo_through(UNITS["gb"][0] + UNITS["gb"][1])
            scale_rows("dsa", sp)
            lo_through(UNITS["kvl"][0] + UNITS["kvl"][1])
            scale_rows("swa", sc2)
            lo_through(UNITS["ukv1"][0] + UNITS["ukv1"][1])
            for h in range(2):
                split_head(h)
            scale_rows("mla", sc2)
            lo_through(len(CHUNKS) - 1)

        @block.scalar
        def _(act):
            nxt = [0]

            def hi_through(c_end):
                for c in range(nxt[0], min(c_end + 1, len(CHUNKS))):
                    n = CHUNKS[c][0] * CHUNKS[c][1]
                    act.wait_ge(w_landed[c % 2], landed[c])
                    if c >= 2:
                        wait_used(act, c - 2)
                    act.activation(w_hi[:, c % 2, 0:n], w_raw[:, c % 2, 0:n], ACT.Copy).then_inc(w_hi_ready, 1)
                    nxt[0] = c + 1

            def ahead(unit):
                first, n, _, _ = UNITS[unit]
                hi_through(first + n)

            def evac(stage, i, dst, src=None, scale=1.0):
                wait_filled(act, stage, i)
                src = bank_of(stage, i)[:] if src is None else src
                empties(act.activation(dst, src, ACT.Copy, scale=scale), stage, i)

            def square(n, j, src):
                base = 8 * (n - 1)
                if base + j >= 2:
                    act.wait_ge(sum_ready, base + j - 1)
                act.activation(sq[:, j % 2, :], src, ACT.Square).then_inc(sq_ready, 1)

            def rms(n):
                wait_filled(act, f"norm{n}", 0)
                empties(act.activation(rT[:], bank_of(f"norm{n}", 0)[:, 0:NB], ACT.Sqrt, scale=1.0 / D, bias=EPS),
                        f"norm{n}", 0)

            def exps(name, sc_, pt, att):
                a = ATT[name]
                scale = MQK ** -0.5 if name == "mla" else DH ** -0.5
                for i in range(NU + LAG_PV + 1):
                    if i > LAG_PV and (i - LAG_PV) % NB == 0:
                        h = (i - LAG_PV) // NB - 1
                        r = slice(DH * (h % 2), DH * (h % 2) + DH)
                        wait_filled(act, name + ".o", h)
                        empties(act.activation(att[r, h // 2, :], bank_of(name + ".o", h)[r, :], ACT.Copy), name + ".o", h)
                    if LAG_HI <= i < NU + LAG_HI:
                        u = i - LAG_HI
                        if u % NB == 0 and u >= 2 * NB:
                            wait_filled(act, name + ".o", u // NB - 2)
                        wait_filled(act, name + ".t", u)
                        act.activation(p_views(a, u, pt, 0), t_view(a, u), ACT.Copy).then_inc(p_hi, 1)
                    if 0 <= i < NU:
                        h, b = a.units[i]
                        k0, k1 = a.keys(b)
                        s = sc_[:, i % RING, 0:(k1 - k0) * P]
                        act.wait_ge(biased, a.index * NU + i + 1)
                        act.activation(s, s, ACT.Exp, bias=nbias[:, i:i + 1], scale=scale,
                                       accum_out=sums[:, i:i + 1]).then_inc(exped, 1)
                        if name == "swa":
                            act.activation(rsum[:, i:i + 1], snk[:, 0, h:h + 1], ACT.Exp,
                                           bias=nbias[:, i:i + 1]).then_inc(sinked, 1)

            def split_high(tm_, st, n_roped):
                act.wait_ge(roped, n_roped)
                for b in range(NB):
                    act.activation(st[:, b, :, 0:DH], tm_[:, b, :].rearrange("p (h d) -> p h d", h=H),
                                   ACT.Copy).then_inc(split_hi, 1)

            def twice_high(dst, src):
                for c in range(2):
                    act.activation(dst[:, :, c * DH:(c + 1) * DH], src, ACT.Copy).then_inc(split_hi, 1)

            act.wait_ge(gains_landed, 16)
            for j in range(KD):
                act.wait_ge(x_landed[j // 2], 16)
                act.activation(aH[:, j, :], xT[:, j, :], ACT.Copy, scale=gv[:, GV["pre"] + j:GV["pre"] + j + 1]).then_inc(a_hi_ready, 1)
                square(1, j, xT[:, j, :])
                if j % 2 == 1 or j == 0:
                    hi_through((j + 1) // 2)
            hi_through(UNITS["sm"][0])
            rms(1)
            act.wait_ge(rt_ready, 1)
            ahead("qi")
            for b in range(NB):
                evac("qi", b, tmI[:, b, :], scale=rT[:, b:b + 1])
            ahead("sm")
            for b in range(NB):
                evac("sm", b, sm[:, b, :], src=bank_of("sm", b)[:, 0:SM_W], scale=rT[:, b:b + 1])
            act.wait_ge(lf_in, 1)
            act.activation(lf[:, 1, :], lf[:, 1, :], ACT.Exp).then_inc(act_step, 1)
            act.wait_ge(act_step, 1)
            act.activation(lf[:, 1, :], lf[:, 1, :], ACT.Ln, bias=1.0).then_inc(lf_ln, 1)
            hi_through(UNITS["sm"][0] + UNITS["sm"][1] + 1)
            split_high(tmI, spI, 1)
            ahead("qb")
            for j in range(NB):
                evac("qb", j, qbT[:, j, :])
            act.wait_ge(roped, 3)
            twice_high(kdI[:, 0], sm[:, :, SM_KI:SM_KI + DH])
            wait_filled(act, "t.ki", 1)
            twice_high(kdI[:, 0], sm[:, :, SM_KA:SM_KA + DH])
            twice_high(vaS[:, 0], sm[:, :, SM_VA:SM_VA + DH])
            for i in range(24):
                h, b = i // 3, 1 + i % 3
                nk = (b + 1) * P
                if i >= RING:
                    act.wait_ge(idx_done, i - RING + 1)
                wait_filled(act, "idx", i)
                empties(act.activation(sp[:, i % RING, 0:nk], bank_of("idx", i)[:, 0:nk], ACT.Relu), "idx", i)
            ahead("kb")
            evac("cum", 0, cT[:, :], src=bank_of("cum", 0)[0:H, :], scale=-8.0)
            for j in range(NB):
                evac("kb", j, kbT[:, j, :])
            ahead("vb")
            for b in range(NB):
                wait_filled(act, "vb", b)
                act.activation(vbS[:, 0, b, :], bank_of("vb", b)[:], ACT.Copy, scale=rT[:, b:b + 1]).then_inc(split_hi, 1)
            hi_through(UNITS["vb"][0] + UNITS["vb"][1])
            exps("fox", sp, pT, attB)
            def silu(g):
                for j in range(NB):
                    act.wait_ge(gate_raw, NB * g + j + 1)
                    t = (gA, gB)[g][:, j, :]
                    act.activation(t, t, ACT.Silu).then_inc(gate_ready, 1)

            ahead("qa")
            for b in range(NB):
                evac("qa", b, tmA[:, b, :], scale=rT[:, b:b + 1])
            ahead("ga")
            for j in range(NB):
                evac("ga", j, gA[:, j, :])
            ahead("gb")
            split_high(tmA, spA, 4)
            silu(0)
            for j in range(NB):
                evac("gb", j, gB[:, j, :])
            for j in range(H):
                evac("t.qa", j, qaS[:, j, :])
            hi_through(UNITS["gb"][0] + UNITS["gb"][1])
            exps("dsa", sp, pT, attA)
            silu(1)
            for i in range(8):
                act.wait_ge(u_mul, i + 1)
                act.activation(uH[:, i, :], tmp[:, i % 2, :], ACT.Copy).then_inc(u_hi_ready, 1)

            def mix(first, names, y, zH, sg, base, u_done):
                for n, (u, t) in enumerate(((names[0] + "0", y[0]), (names[0] + "1", y[0]),
                                            (names[1] + "0", y[1]), (names[1] + "1", y[1]))):
                    ahead(u)
                    for j in range(NB):
                        evac(u, j, t[:, 4 * (n % 2) + j, :])
                for n in range(4):
                    ahead(f"{names[2]}{n}")
                    for j in range(NB):
                        wait_emptied(act, f"{names[2]}{n}", j)
                        act.activation(sg[:, j % 2, :], sg[:, j % 2, :], ACT.Sigmoid).then_inc(sg_ready, 1)
                        if n >= 2:
                            t = 4 * (n - 2) + j
                            if t >= 1:
                                hi_z(t - 1, y, zH, base)
                hi_z(7, y, zH, base)

            def hi_z(t, y, zH, base):
                act.wait_ge(z_ready, base + t + 1)
                act.activation(zH[:, t, :], y[0][:, t, :], ACT.Copy).then_inc(u_hi_ready, 1)

            mix(None, ("ya", "yb", "m"), (yA, yB), uH, sg, 0, None)
            for j in range(2):
                act.wait_ge(p_landed, 16)
                act.activation(pH[:, j, :], pr[:, j, :], ACT.Copy).then_inc(p_hi_ready, 1)
            for n in range(2):
                ahead(f"wo{n}")
                for j in range(NB):
                    t = 4 * n + j
                    evac(f"wo{n}", j, oT[:, t, :])
                    wait_emptied(act, f"wo{n}", j)
                    square(2, t, oT[:, t, :])
            hi_through(UNITS["e1"][0])
            rms(2)
            ahead("e0")
            for j in range(NB):
                evac("e0", j, eT[:, j, :])
            hi_through(UNITS["pg0"][0])
            for j in range(KD):
                act.wait_ge(x_new, j + 1)
                act.activation(aH[:, j, :], xT[:, j, :], ACT.Copy).then_inc(a_hi_ready, 1)
                if j == 1:
                    for i in range(NB):
                        evac("e1", i, eT[:, 4 + i, :])
                if j == 2:
                    hi_through(UNITS["pg0"][0] + 1)
            for n in range(2):
                ahead(f"pg{n}")
                for j in range(NB):
                    t = 4 * n + j
                    if t >= 2:
                        act.wait_ge(y_ready, t - 1)
                    wait_filled(act, f"pg{n}", j)
                    empties(act.activation(sg[:, t % 2, :], bank_of(f"pg{n}", j)[:], ACT.Sigmoid), f"pg{n}", j)
                    if t >= 1:
                        act.wait_ge(y_ready, t)
                        square(3, t - 1, oT[:, t - 1, :])
            act.wait_ge(y_ready, 8)
            square(3, 7, oT[:, 7, :])
            rms(3)
            hi_through(UNITS["sq"][0] + 1)
            for j in range(KD):
                act.wait_ge(x_new, 8 + j + 1)
                act.activation(aH[:, j, :], xT[:, j, :], ACT.Copy, scale=gv[:, GV["mix"] + j:GV["mix"] + j + 1]).then_inc(a_hi_ready, 1)
                square(4, j, xT[:, j, :])
            hi_through(UNITS["skv"][0])
            rms(4)
            act.wait_ge(rt_ready, 4)
            ahead("sq")
            for b in range(NB):
                evac("sq", b, tm2[:, b, :], scale=rT[:, b:b + 1])
            ahead("skv")
            for b in range(NB):
                evac("skv", b, skv[:, b, :], src=bank_of("skv", b)[:, 0:256], scale=rT[:, b:b + 1])
            hi_through(UNITS["skv"][0] + UNITS["skv"][1] + 1)
            split_high(tm2, sp2, 4 + NB)
            act.wait_ge(roped, 4 + 2 * NB)
            for kv in range(2):
                twice_high(kd2[:, kv, 0], skv[:, :, kv * DH:(kv + 1) * DH])
            for kv in range(2):
                twice_high(vsS[:, 0, kv], skv[:, :, (2 + kv) * DH:(3 + kv) * DH])
            for n, (u, t, w) in enumerate((("ql", ql, QR), ("kvl", kvl, KVR))):
                ahead(u)
                full = CHUNKS[UNITS[u][0]][1]
                for b in range(NB):
                    evac(u, b, t[:, b, :], src=bank_of(u, b)[:, 0:full], scale=rT[:, b:b + 1])
                for b in range(NB):
                    wait_emptied(act, u, b)
                    if 4 * n + b >= 2:
                        act.wait_ge(ql_sq, 4 * n + b - 1)
                    act.activation(sq[:, b % 2, 0:w], t[:, b, 0:w], ACT.Square,
                                   accum_out=qs[:, n, b:b + 1]).then_inc(ql_sq, 1)
                act.wait_ge(ql_sq, 4 * n + 4)
                act.activation(qs[:, n, 4:8], qs[:, n, 0:4], ACT.Sqrt, scale=1.0 / w, bias=EPS).then_inc(ql_r, 1)
            for stage, tiles, dst, g, base in (("t.cq", 3, cqH, "q", 0), ("t.ck", 2, ckH, "kv", 3)):
                for j in range(tiles):
                    wait_filled(act, stage, j)
                    act.activation(dst[:, j, :], bank_of(stage, j)[:], ACT.Copy,
                                   scale=gv[:, GV[g] + j:GV[g] + j + 1]).then_inc(c_hi_ready, 1)
            hi_through(UNITS["kvl"][0] + UNITS["kvl"][1])
            exps("swa", sc2, pT2, oA)
            wait_emptied(act, "swa.t", NU - 1)
            for i in range(2):
                ahead(f"uq{i}")
                for b in range(NB):
                    evac(f"uq{i}", b, uq[i][:, b, :], src=bank_of(f"uq{i}", b)[:, 0:QR])
                ahead(f"ukv{i}")
                for b in range(NB):
                    src = bank_of(f"ukv{i}", b)[:].rearrange("p (h d) -> p h d", h=4)
                    wait_filled(act, f"ukv{i}", b)
                    act.activation(mk[i][:, b, :, 0:DH], src[:, :, 0:DH], ACT.Copy).then_inc(mk_ready, 1)
                    act.activation(mvS[:, 0, b, 4 * i:4 * i + 4, :], src[:, :, DH:2 * DH], ACT.Copy).then_inc(split_hi, 1)
            wait_emptied(act, "t.mk1", 3)
            hi_through(UNITS["ukv1"][0] + UNITS["ukv1"][1])
            exps("mla", sc2, pT2, oB)
            for i in range(8):
                o = (oA, oB)[i // 4]
                act.wait_ge(*att_done("swa" if i < 4 else "mla"))
                act.activation(uH2[:, i, :], o[:, i % 4, :], ACT.Copy).then_inc(u_hi_ready, 1)
            mix(None, ("za", "zb", "n"), (yA2, yB2), uH2, sg2, 8, None)
            for j in range(KD):
                if j % 4 == 0:
                    ahead(f"wp{j // 4}")
                wait_emptied(act, f"wp{j // 4}", j % 4)
                act.activation(aH[:, j, :], xT[:, j, :], ACT.Copy, scale=gv[:, GV["ffn"] + j:GV["ffn"] + j + 1]).then_inc(a_hi_ready, 1)
                square(5, j, xT[:, j, :])
            hi_through(UNITS["f1"][0])
            rms(5)
            for f in range(DFF // 256):
                ahead(f"f{f}")
                for j in range(2):
                    wait_emptied(act, f"f{f}", j)
                    act.activation(fg[:, j, :], fg[:, j, :], ACT.Silu).then_inc(ff_act, 1)
                for j in range(2):
                    t = 2 * f + j
                    act.wait_ge(ff_prod, t + 1)
                    act.activation(fH[:, t, :], fg[:, j, :], ACT.Copy).then_inc(ff_hi, 1)
            for i in range(0, 8, 2):
                if i == 0:
                    wait_filled(act, "xr", 7)
                evac("xr", i, xr[:, i // 2, 512 * (i % 2):512 * (i % 2) + 512])
            hi_through(len(CHUNKS) - 1)
            for b in range(NB):
                act.wait_ge(fin_sq, b + 1)
                act.activation(sq[:, :, :].rearrange("p a b -> p (a b)"), xr[:, b, :], ACT.Square,
                               accum_out=qs[:, 0, b:b + 1]).then_inc(act_step, 1)
                act.wait_ge(act_step, 2 + 2 * b)
                act.activation(qs[:, 1, b:b + 1], qs[:, 0, b:b + 1], ACT.Sqrt, scale=1.0 / D, bias=EPS).then_inc(act_step, 1)


        @block.vector
        def _(dve):
            steps, ropes = [0], [0]

            def link(ins):
                steps[0] += 1
                ins.then_inc(dve_step, 1)
                dve.wait_ge(dve_step, steps[0])

            def mult(o, a, b):
                return dve.tensor_tensor(out=o, in0=a, in1=b, op=ALU.mult)

            def add_sq(n, j):
                base = 8 * (n - 1)
                dve.wait_ge(sq_ready, base + j + 1)
                if j == 0:
                    if n > 1:
                        wait_filled(dve, f"norm{n - 1}", 0)
                    dve.tensor_copy(ssum[:], sq[:, 0, :]).then_inc(sum_ready, 1)
                else:
                    dve.wait_ge(sum_ready, base + j)
                    dve.tensor_tensor(out=ssum[:], in0=ssum[:], in1=sq[:, j % 2, :], op=ALU.add).then_inc(sum_ready, 1)

            def rms(n):
                wait_emptied(dve, f"norm{n}", 0)
                dve.reciprocal(rT[:], rT[:]).then_inc(rt_ready, 1)
                dve.wait_ge(rt_ready, n)
                for b in range(NB):
                    ins = dve.tensor_scalar(rB[:, b * P:(b + 1) * P], ident[:], rT[:, b:b + 1], None, ALU.mult)
                ins.then_inc(diag_ready, 1)
                wait_filled(dve, f"norm{n}", 1)
                empties(dve.tensor_copy(rB[:], bank_of(f"norm{n}", 1)[:]), f"norm{n}", 1)
                wait_emptied(dve, f"norm{n}", 1)

            def rope(x, shape, half, cos, sin, t0, t1):
                x1, x2 = x[..., 0:half], x[..., half:2 * half]
                mult(t0, x2, sin)
                mult(t1, x1, sin)
                mult(x1, x1, cos)
                link(mult(x2, x2, cos))
                dve.tensor_tensor(out=x1, in0=x1, in1=t0, op=ALU.subtract)
                dve.tensor_tensor(out=x2, in0=x2, in1=t1, op=ALU.add).then_inc(roped, 1)
                ropes[0] += 1
                dve.wait_ge(roped, ropes[0])

            def rope_blocks(x, heads, half, which, rp):
                cos, sin = (rope_tab(n + which, half).rearrange("p b (o f) -> p b o f", o=1)
                            .broadcast_to([P, NB, heads, half]) for n in ("cos", "sin"))
                n = NB * heads * half
                t0, t1 = (rp[:, i, 0:n].rearrange("p (b h f) -> p b h f", b=NB, h=heads) for i in range(2))
                rope(x, None, half, cos, sin, t0, t1)

            def rope_block(x, b, heads, half, which, rp):
                cos, sin = (rope_tab(n + which, half)[:, b:b + 1, :].broadcast_to([P, heads, half])
                            for n in ("cos", "sin"))
                n = heads * half
                t0, t1 = (rp[:, i, 0:n].rearrange("p (h f) -> p h f", h=heads) for i in range(2))
                rope(x, None, half, cos, sin, t0, t1)

            def evac(stage, i, dst, src=None):
                wait_filled(dve, stage, i)
                empties(dve.tensor_copy(dst, bank_of(stage, i)[:] if src is None else src), stage, i)

            def softmax(name, sc_, pt, k_bias):
                a = ATT[name]
                scale = MQK ** -0.5 if name == "mla" else DH ** -0.5
                for i in range(NU + LAG_LO):
                    if 0 <= i < NU:
                        h, b = a.units[i]
                        k0, k1 = a.keys(b)
                        n = (k1 - k0) * P
                        if i >= RING:
                            wait_filled(dve, name + ".t", i - RING)
                        wait_filled(dve, name + ".l", i)
                        empties(dve.tensor_tensor_reduce(
                            out=sc_[:, i % RING, 0:n], in0=bank_of(name + ".l", i)[:, 0:n], in1=k_bias(h, b),
                            scale=1.0, scalar=-3e38, op0=ALU.add, op1=ALU.max, accum_out=mx[:, i:i + 1]),
                            name + ".l", i)
                    if LAG_R <= i < NU + LAG_R:
                        c = slice(i - LAG_R, i - LAG_R + 1)
                        dve.wait_ge(exped, a.index * NU + i - LAG_R + 1)
                        if name == "swa":
                            dve.wait_ge(sinked, i - LAG_R + 1)
                            link(dve.tensor_tensor(out=sums[:, c], in0=sums[:, c], in1=rsum[:, c], op=ALU.add))
                        dve.reciprocal(rsum[:, c], sums[:, c]).then_inc(row_inv, 1)
                    if 0 <= i < NU:
                        wait_emptied(dve, name + ".l", i)
                        if name == "swa":
                            dve.tensor_scalar(nbias[:, i:i + 1], mx[:, i:i + 1], -scale, snk[:, 1, h:h + 1],
                                              ALU.mult, ALU.min).then_inc(biased, 1)
                        else:
                            dve.tensor_scalar(nbias[:, i:i + 1], mx[:, i:i + 1], -scale, None,
                                              ALU.mult).then_inc(biased, 1)
                    if i >= LAG_LO:
                        u = i - LAG_LO
                        dve.wait_ge(p_hi, a.index * NU + u + 1)
                        empties(dve.tensor_tensor(out=p_views(a, u, pt, 1), in0=t_view(a, u),
                                                  in1=p_views(a, u, pt, 0).bitcast(F32), op=ALU.subtract),
                                name + ".t", u)
                    if name == "fox" and i in PAIR_HI_AT:
                        split_pair(PAIR_HI_AT[i])
                    if name == "mla" and i < NU and i % NB == NB - 1 and i // NB + 2 < H:
                        split_head(i // NB + 2)

            def split_pair(j):
                if j:
                    for h in range(2):
                        dve.wait_ge(head_landed[h], 96 * (2 if j == 3 else 1))
                for p, t in enumerate((qbT, kbT)):
                    dve.tensor_copy(pair_hi(p, j), t[:, j, :]).then_inc(pair_hi_ready, 1)

            def split_head(h):
                if h >= 2:
                    wait_filled(dve, "mla.l", NB * (h - 1) - 1)
                for t, m_ in ((mqT, mQ), (mkT, mK)):
                    dve.tensor_copy(m_[0:MQK, h % 2, 0, :], t[0:MQK, h, :]).then_inc(mla_hi_ready, 1)

            splits = [0]

            def split_low(tm_, st):
                for b in range(NB):
                    splits[0] += 1
                    dve.wait_ge(split_hi, splits[0])
                    dve.tensor_tensor(out=st[:, b, :, DH:P], in0=tm_[:, b, :].rearrange("p (h d) -> p h d", h=H),
                                      in1=st[:, b, :, 0:DH].bitcast(F32), op=ALU.subtract).then_inc(split_lo, 1)

            def twice_low(dst, hi, src):
                splits[0] += 2
                dve.wait_ge(split_hi, splits[0])
                for c in range(2):
                    dve.tensor_tensor(out=dst[:, :, c * DH:(c + 1) * DH], in0=src,
                                      in1=hi[:, :, c * DH:(c + 1) * DH].bitcast(F32), op=ALU.subtract).then_inc(split_lo, 1)

            def mix(names, y, zH, zL, sg, base):
                def prod(q):
                    dve.wait_ge(sg_ready, 2 * base + q + 1)
                    if q < 8:
                        wait_emptied(dve, f"{names[0]}{q // 4}", q % 4)
                        link(mult(y[0][:, q, :], sg[:, q % 2, :], y[0][:, q, :]))
                        return
                    t = q - 8
                    wait_emptied(dve, f"{names[1]}{t // 4}", t % 4)
                    link(mult(y[1][:, t, :], sg[:, q % 2, :], y[1][:, t, :]))
                    dve.tensor_tensor(out=y[0][:, t, :], in0=y[0][:, t, :], in1=y[1][:, t, :],
                                      op=ALU.add).then_inc(z_ready, 1)

                def low(t):
                    dve.wait_ge(u_hi_ready, 2 * base + 8 + t + 1)
                    dve.tensor_tensor(out=zL[:, t, :], in0=y[0][:, t, :], in1=zH[:, t, :].bitcast(F32),
                                      op=ALU.subtract).then_inc(u_lo_ready, 1)

                for q in range(18):
                    if q < 16:
                        n, j = q // 4, q % 4
                        wait_filled(dve, f"{names[2]}{n}", j)
                        empties(mult(sg[:, q % 2, :], bank_of(f"{names[2]}{n}", j)[:], rB[:]), f"{names[2]}{n}", j)
                    if 1 <= q <= 16:
                        prod(q - 1)
                    if q >= 10:
                        low(q - 10)

            dve.wait_ge(gains_landed, 16)
            for j in range(KD):
                dve.wait_ge(a_hi_ready, j + 1)
                dve.scalar_tensor_tensor(out=aL[:, j, :], in0=xT[:, j, :], scalar=gv[:, GV["pre"] + j:GV["pre"] + j + 1],
                                         in1=aH[:, j, :].bitcast(F32), op0=ALU.mult, op1=ALU.subtract).then_inc(a_lo_ready, 1)
                add_sq(1, j)
            rms(1)
            dve.wait_ge(cst_landed, 32)
            dve.tensor_copy(ident16[:], ident[:])
            dve.tensor_copy(diag16[:], tab("causal")[:, 3 * P:4 * P]).then_inc(half_ready, 1)
            dve.wait_ge(small_landed, 32)
            tm4 = tmI[:, :, :].rearrange("p b (h d) -> p b h d", h=H)
            for b in range(NB):
                wait_emptied(dve, "qi", b)
            rope_blocks(tm4, H, 8, "1", rp)
            for b in range(NB):
                wait_emptied(dve, "sm", b)
            z = lf[:, 0, :].rearrange("p (b h) -> p b h", b=NB)
            link(dve.tensor_tensor(out=z, in0=sm[:, :, SM_FB:SM_FB + H],
                                   in1=bfg[:, :].rearrange("p (o h) -> p o h", o=1).broadcast_to([P, NB, H]), op=ALU.add))
            dve.scalar_tensor_tensor(out=lf[:, 1, :], in0=lf[:, 0, :], scalar=-1.0, in1=lf[:, 0, :],
                                     op0=ALU.mult, op1=ALU.min).then_inc(lf_in, 1)
            for o in (SM_KI, SM_KA):
                rope_blocks(sm[:, :, o:o + DH].rearrange("p b (h d) -> p b h d", h=1), 1, 8, "1", rp)
            split_low(tmI, spI)
            twice_low(kdI[:, 1], kdI[:, 0], sm[:, :, SM_KI:SM_KI + DH])
            link(dve.tensor_scalar(sm[:, :, SM_WI:SM_WI + H], sm[:, :, SM_WI:SM_WI + H], (H ** -0.5) * (DH ** -0.5),
                                   None, ALU.mult))
            link(dve.tensor_scalar(lf[:, 2, :], lf[:, 0, :], 0.0, None, ALU.min))
            for j in range(H):
                evac("t.qi", j, qiS[:, j, :])
            for j in range(2):
                evac("t.ki", j, kiS[:, j, :])
            twice_low(kdI[:, 1], kdI[:, 0], sm[:, :, SM_KA:SM_KA + DH])
            twice_low(vaS[:, 1], vaS[:, 0], sm[:, :, SM_VA:SM_VA + DH])
            dve.wait_ge(lf_ln, 1)
            dve.tensor_tensor(out=lf[:, 3, :], in0=lf[:, 2, :], in1=lf[:, 1, :], op=ALU.subtract).then_inc(logf_ready, 1)

            span = {1: (0, 2 * P), 2: (2 * P, 5 * P), 3: (5 * P, 9 * P)}
            for i in range(24):
                h, b = i // 3, 1 + i % 3
                lo, hi = span[b]
                dve_in = sp[:, i % RING, 0:hi - lo]
                w = sm[:, b, SM_WI + h:SM_WI + h + 1]
                wait_emptied(dve, "idx", i)
                if h == 0:
                    dve.tensor_scalar(sc[:, lo:hi], dve_in, w, None, ALU.mult).then_inc(idx_done, 1)
                else:
                    dve.wait_ge(idx_done, i - 2)
                    dve.scalar_tensor_tensor(out=sc[:, lo:hi], in0=dve_in, scalar=w, in1=sc[:, lo:hi],
                                             op0=ALU.mult, op1=ALU.add).then_inc(idx_done, 1)
            dve.wait_ge(idx_done, 24)
            for b in range(1, NB):
                lo, hi = span[b]
                ins = dve.tensor_tensor(out=sc[:, hi - P:hi], in0=sc[:, hi - P:hi], in1=tab("causal")[:, 3 * P:4 * P],
                                        op=ALU.add)
            link(ins)
            for j in range(2):
                evac("t.ka", j, kaS[:, j, :])
            def top_rounds(n):
                for r in range(n):
                    for b in range(1, NB):
                        lo, hi = span[b]
                        ins = dve.max(out=m8[:, b - 1, :], in_=sc[:, lo:hi])
                    link(ins)
                    for b in range(1, NB):
                        lo, hi = span[b]
                        ins = dve.match_replace(out=sc[:, lo:hi], in_to_replace=m8[:, b - 1, :], in_values=sc[:, lo:hi],
                                                imm_value=TAKEN)
                    link(ins)

            top_rounds(ROUNDS_FIRST)

            dve.wait_ge(qb_scaled, 8)
            dve.wait_ge(cum_stored, 16)
            split_pair(0)
            for b in range(NB):
                splits[0] += 1
                dve.wait_ge(split_hi, splits[0])
                empties(dve.scalar_tensor_tensor(out=vbS[:, 1, b, :], in0=bank_of("vb", b)[:], scalar=rT[:, b:b + 1],
                                                 in1=vbS[:, 0, b, :].bitcast(F32), op0=ALU.mult, op1=ALU.subtract), "vb", b)

            def fox_bias(h, b):
                if b == 0:
                    dve.wait_ge(cum_landed[h % 2], 16 * (h // 2 + 1))
                return cB[:, h % 2, 0:(b + 1) * P]

            softmax("fox", sp, pT, fox_bias)
            top_rounds(TOPK // 8 - ROUNDS_FIRST)
            link(dve.tensor_scalar(sc[:], sc[:], TAKEN * 0.9, NEG, ALU.is_gt, ALU.mult))
            for b in range(NB):
                wait_emptied(dve, "qa", b)
            rope_blocks(tmA[:, :, :].rearrange("p b (h d) -> p b h d", h=H), H, 8, "1", rp)
            split_low(tmA, spA)
            softmax("dsa", sp, pT,
                    lambda h, b: tab("causal")[:, 3 * P:4 * P] if b == 0 else sc[:, span[b][0]:span[b][1]])
            dve.wait_ge(*att_done("fox"))
            dve.wait_ge(*att_done("dsa"))
            for i in range(9):
                if i < 8:
                    att, g = ((attA, gA), (attB, gB))[i // 4]
                    if i >= 2:
                        dve.wait_ge(u_lo_ready, i - 1)
                    dve.wait_ge(gate_ready, i + 1)
                    mult(tmp[:, i % 2, :], att[:, i % 4, :], g[:, i % 4, :]).then_inc(u_mul, 1)
                if i >= 1:
                    dve.wait_ge(u_hi_ready, i)
                    dve.tensor_tensor(out=uL[:, i - 1, :], in0=tmp[:, (i - 1) % 2, :],
                                      in1=uH[:, i - 1, :].bitcast(F32), op=ALU.subtract).then_inc(u_lo_ready, 1)
            mix(("ya", "yb", "m"), (yA, yB), uH, uL, sg, 0)
            for j in range(2):
                dve.wait_ge(p_hi_ready, j + 1)
                dve.tensor_tensor(out=pL[:, j, :], in0=pr[:, j, :], in1=pH[:, j, :].bitcast(F32),
                                  op=ALU.subtract).then_inc(p_lo_ready, 1)

            def residual(n, gname, after, gnext):
                for j in range(9):
                    if j < 8:
                        g = gv[:, GV[gname] + j:GV[gname] + j + 1]
                        link(dve.scalar_tensor_tensor(out=tmp[:, j % 2, :], in0=oT[:, j, :], scalar=g, in1=rB[:],
                                                      op0=ALU.mult, op1=ALU.mult))
                        dve.tensor_tensor(out=xT[:, j, :], in0=xT[:, j, :], in1=tmp[:, j % 2, :],
                                          op=ALU.add).then_inc(x_new, 1)
                    if j >= 1:
                        low_x(n, j - 1, gnext)
                        if after:
                            add_sq(after, j - 1)

            def low_x(n, j, gnext):
                dve.wait_ge(a_hi_ready, 8 * n + j + 1)
                g = 1.0 if gnext is None else gv[:, GV[gnext] + j:GV[gnext] + j + 1]
                dve.scalar_tensor_tensor(out=aL[:, j, :], in0=xT[:, j, :], scalar=g, in1=aH[:, j, :].bitcast(F32),
                                         op0=ALU.mult, op1=ALU.subtract).then_inc(a_lo_ready, 1)

            for j in range(8):
                add_sq(2, j)
            rms(2)
            dve.wait_ge(x_back, 16)
            residual(1, "post", None, None)
            for t in range(9):
                if t < 8:
                    wait_emptied(dve, f"e{t // 4}", t % 4)
                    wait_emptied(dve, f"pg{t // 4}", t % 4)
                    mult(oT[:, t, :], sg[:, t % 2, :], eT[:, t, :]).then_inc(y_ready, 1)
                if t >= 1:
                    add_sq(3, t - 1)
            rms(3)
            residual(2, "ple", 4, "mix")
            rms(4)

            dve.wait_ge(small_landed, 32)
            link(dve.tensor_scalar(snk[:, 1, :], snk[:, 0, :], -1.0, None, ALU.mult))
            for b in range(NB):
                wait_emptied(dve, "sq", b)
                rope_block(tm2[:, b, :].rearrange("p (h d) -> p h d", h=H), b, H, 32, "2", rp2)
            for b in range(NB):
                wait_emptied(dve, "skv", b)
                rope_block(skv[:, b, 0:2 * DH].rearrange("p (h d) -> p h d", h=2), b, 2, 32, "2", rp2)
            split_low(tm2, sp2)
            for kv in range(2):
                twice_low(kd2[:, kv, 1], kd2[:, kv, 0], skv[:, :, kv * DH:(kv + 1) * DH])
            for kv in range(2):
                twice_low(vsS[:, 1, kv], vsS[:, 0, kv], skv[:, :, (2 + kv) * DH:(3 + kv) * DH])
            for j in range(H):
                evac("t.sq", j, sqS[:, j, :])
            for j in range(4):
                evac("t.sk", j, skS[:, j // 2, j % 2, :])
            for n, (t, w) in enumerate(((ql, QR), (kvl, KVR))):
                dve.wait_ge(ql_r, n + 1)
                link(dve.reciprocal(qs[:, n, 4:8], qs[:, n, 4:8]))
                for b in range(NB):
                    dve.tensor_scalar(t[:, b, 0:w], t[:, b, 0:w], qs[:, n, 4 + b:5 + b], None,
                                      ALU.mult).then_inc(ql_scaled, 1)
            rope_blocks(kvl[:, :, KVR:KVR + MR].rearrange("p b (h d) -> p b h d", h=1), 1, 16, "3", rp2)
            for stage, tiles, hi, lo, g, base in (("t.cq", 3, cqH, cqL, "q", 0), ("t.ck", 2, ckH, ckL, "kv", 3)):
                for j in range(tiles):
                    dve.wait_ge(c_hi_ready, base + j + 1)
                    empties(dve.scalar_tensor_tensor(
                        out=lo[:, j, :], in0=bank_of(stage, j)[:], scalar=gv[:, GV[g] + j:GV[g] + j + 1],
                        in1=hi[:, j, :].bitcast(F32), op0=ALU.mult, op1=ALU.subtract), stage, j)
            dve.wait_ge(x_stored, 16)
            softmax("swa", sc2, pT2, lambda h, b: tab("band")[:, P:2 * P] if b == 0 else tab("band"))
            dve.wait_ge(*att_done("swa"))
            wait_emptied(dve, "swa.t", NU - 1)
            for i in range(2):
                for b in range(NB):
                    kr = kvl[:, b, KVR:KVR + MR].rearrange("p (o d) -> p o d", o=1).broadcast_to([P, 4, MR])
                    ins = dve.tensor_copy(mk[i][:, b, :, DH:MQK], kr)
                ins.then_inc(kr_copied, 1)
            for i in range(2):
                for b in range(NB):
                    wait_emptied(dve, f"uq{i}", b)
                uq4 = uq[i][:, :, :].rearrange("p b (h d) -> p b h d", h=4)
                rope_blocks(uq4[:, :, :, DH:MQK], 4, 16, "3", rp3)
                if i == 1:
                    for j in range(4):
                        evac("t.mk0", j, mkT[0:MQK, j, :], src=bank_of("t.mk0", j)[0:MQK, :])
                    wait_emptied(dve, "t.mk0", 3)
                    for h in range(2):
                        split_head(h)
                for b in range(NB):
                    splits[0] += 1
                    dve.wait_ge(split_hi, splits[0])
                    src = bank_of(f"ukv{i}", b)[:].rearrange("p (h d) -> p h d", h=4)
                    empties(dve.tensor_tensor(out=mvS[:, 1, b, 4 * i:4 * i + 4, :], in0=src[:, :, DH:2 * DH],
                                              in1=mvS[:, 0, b, 4 * i:4 * i + 4, :].bitcast(F32), op=ALU.subtract), f"ukv{i}", b)
                for j in range(4):
                    evac(f"t.mq{i}", j, mqT[0:MQK, 4 * i + j, :], src=bank_of(f"t.mq{i}", j)[0:MQK, :])
            for j in range(4):
                evac("t.mk1", j, mkT[0:MQK, 4 + j, :], src=bank_of("t.mk1", j)[0:MQK, :])
            wait_emptied(dve, "t.mk1", 3)
            softmax("mla", sc2, pT2, lambda h, b: tab("causal")[:, (3 - b) * P:4 * P])
            for i in range(8):
                o = (oA, oB)[i // 4]
                dve.wait_ge(u_hi_ready, 16 + i + 1)
                dve.tensor_tensor(out=uL2[:, i, :], in0=o[:, i % 4, :], in1=uH2[:, i, :].bitcast(F32),
                                  op=ALU.subtract).then_inc(u_lo_ready, 1)
            mix(("za", "zb", "n"), (yA2, yB2), uH2, uL2, sg2, 8)
            dve.wait_ge(x_back, 32)
            for j in range(9):
                if j < 8:
                    wait_filled(dve, f"wp{j // 4}", j % 4)
                    empties(dve.tensor_tensor(out=xT[:, j, :], in0=bank_of(f"wp{j // 4}", j % 4)[:], in1=xT[:, j, :],
                                              op=ALU.add), f"wp{j // 4}", j % 4)
                if j >= 1:
                    low_x(3, j - 1, "ffn")
                    add_sq(5, j - 1)
            rms(5)
            for f in range(DFF // 256):
                if f:
                    dve.wait_ge(ff_lo, 2 * f)
                for j in range(2):
                    wait_filled(dve, f"f{f}", j)
                    empties(mult(fg[:, j, :], bank_of(f"f{f}", j)[:], rB[:]), f"f{f}", j)
                for j in range(2):
                    wait_filled(dve, f"f{f}", 2 + j)
                    empties(mult(fu[:, j, :], bank_of(f"f{f}", 2 + j)[:], rB[:]), f"f{f}", 2 + j)
                    wait_emptied(dve, f"f{f}", 2 + j)
                    dve.wait_ge(ff_act, 2 * f + j + 1)
                    mult(fg[:, j, :], fg[:, j, :], fu[:, j, :]).then_inc(ff_prod, 1)
                for j in range(2):
                    t = 2 * f + j
                    dve.wait_ge(ff_hi, t + 1)
                    dve.tensor_tensor(out=fL[:, t, :], in0=fg[:, j, :], in1=fH[:, t, :].bitcast(F32),
                                      op=ALU.subtract).then_inc(ff_lo, 1)
            for i in range(1, 8, 2):
                if i == 1:
                    wait_filled(dve, "xr", 7)
                evac("xr", i, xr[:, i // 2, 512 * (i % 2):512 * (i % 2) + 512])
            dve.wait_ge(small_landed, 48)
            for step in range(NB + 1):
                if step < NB:
                    for half in range(2):
                        i = 2 * step + half
                        part = xr[:, step, 512 * half:512 * half + 512]
                        wait_emptied(dve, "xr", i)
                        wait_filled(dve, "down", i)
                        ins = dve.tensor_tensor(out=part, in0=bank_of("down", i)[:], in1=part, op=ALU.add)
                    ins.then_inc(fin_sq, 1)
                if step >= 1:
                    b = step - 1
                    dve.wait_ge(act_step, 3 + 2 * b)
                    link(dve.reciprocal(qs[:, 1, 4 + b:5 + b], qs[:, 1, b:b + 1]))
                    dve.scalar_tensor_tensor(out=xr[:, b, :], in0=xr[:, b, :], scalar=qs[:, 1, 4 + b:5 + b], in1=gfin[:],
                                             op0=ALU.mult, op1=ALU.mult).then_inc(fin_ready, 1)

        @block.tensor
        def _(pe):
            def open_bank(stage, i):
                b, n = USE[stage][i]
                if n:
                    pe.wait_ge(emptied[b], n)
                return bank[b]

            def fills(ins, stage, i):
                ins.then_inc(filled[USE[stage][i][0]], 1)

            def gemm(unit, in_hi, in_lo, token_major, in_ready=None, between=None, k_first=0, by_rows=False):
                first, n_chunks, _, _ = UNITS[unit]
                for c in range(first, first + n_chunks):
                    if c != first + n_chunks - 1 or by_rows:
                        for k in range(CHUNKS[c][0]):
                            if between and CHUNKS[c][3] + k == UNITS[unit][2] - 1:
                                between()
                            for j in range(4):
                                part(unit, c, j, in_hi, in_lo, token_major, in_ready, k_first, k, k + 1)
                    else:
                        for j in range(4):
                            part(unit, c, j, in_hi, in_lo, token_major, in_ready, k_first, 0, CHUNKS[c][0])

            def part(unit, c, j, in_hi, in_lo, token_major, in_ready, k_first, k0, k1):
                first, n_chunks, total, n = UNITS[unit]
                if k0 == 0 and j == 0:
                    pe.wait_ge(w_hi_ready, c + 1)
                    pe.wait_ge(w_lo_ready, c + 1)
                if c == first and k0 == 0:
                    open_bank(unit, j)
                out_b = bank_of(unit, j)
                wh, wl = w_view(w_hi, c), w_view(w_lo, c)
                for k in range(k0, k1):
                    kk = CHUNKS[c][3] + k
                    if in_ready and j == 0:
                        in_ready(kk)
                    ah, al = in_hi[:, k_first + kk, :], in_lo[:, k_first + kk, :]
                    if token_major:
                        tok = slice(j * P, (j + 1) * P)
                        o = out_b[:, 0:n]
                        pairs = ((ah[:, tok], wh[:, k, :]), (ah[:, tok], wl[:, k, :]), (al[:, tok], wh[:, k, :]))
                    else:
                        col = slice(j * P, (j + 1) * P)
                        o = out_b[:, :]
                        pairs = ((wh[:, k, col], ah), (wh[:, k, col], al), (wl[:, k, col], ah))
                    for m, (l, r) in enumerate(pairs):
                        ins = pe.matmul(o, l, r, start=(kk == 0 and m == 0), stop=(kk == total - 1 and m == 2),
                                        skip_group_check=True)
                if kk == total - 1:
                    fills(ins, unit, j)
                elif j == 3 and k1 == CHUNKS[c][0]:
                    ins.then_inc(w_used, 1)

            def norm(n):
                pe.wait_ge(sum_ready, 8 * n)
                o = open_bank(f"norm{n}", 0)
                for b in range(NB):
                    ins = pe.matmul(o[:, b:b + 1], ssum[:, b * P:(b + 1) * P], ones[:, 0:1], start=True, stop=True)
                fills(ins, f"norm{n}", 0)

            def spread(n):
                pe.wait_ge(diag_ready, n)
                o = open_bank(f"norm{n}", 1)
                fills(pe.matmul(o[:], ones[:], rB[:], start=True, stop=True), f"norm{n}", 1)

            def turn_tile(stage, i, src, rows=P):
                o = open_bank(stage, i)
                for b in range(NB):
                    ins = pe.transpose(o[0:rows, b * P:(b + 1) * P], src(b), ident[:])
                fills(ins, stage, i)

            def attention(name, scores, values, sc_, pt, v_stage=None):
                a = ATT[name]
                for i in range(NU + LAG_PV + 1):
                    if i < NU:
                        h, b = a.units[i]
                        k0, k1 = a.keys(b)
                        if b == 0 and name == "fox":
                            pe.wait_ge(head_landed[h % 2], 96 * (h // 2 + 1))
                        if b == 0 and name == "mla":
                            pe.wait_ge(mla_lo_ready, 2 * h + 2)
                        o = open_bank(name + ".l", i)[:, 0:(k1 - k0) * P]
                        pairs = scores(h, slice(b * P, (b + 1) * P), slice(k0 * P, k1 * P))
                        for m, (q, k) in enumerate(pairs):
                            ins = pe.matmul(o, q, k, start=(m == 0), stop=(m == len(pairs) - 1))
                        if name == "fox":
                            ins = pe.matmul(o[:, b * P:(b + 1) * P], ident16[:], diag16[:], start=False, stop=True,
                                            skip_group_check=True)
                        fills(ins, name + ".l", i)
                    if LAG_T <= i < NU + LAG_T:
                        u = i - LAG_T
                        h, b = a.units[u]
                        k0, k1 = a.keys(b)
                        pe.wait_ge(scaled, a.index * NU + u + 1)
                        o = open_bank(name + ".t", u)
                        for at, kb in enumerate(p_order(a, h, b)):
                            src = sc_[:, u % RING, (kb - k0) * P:(kb - k0 + 1) * P]
                            ins = pe.transpose(o[:, at * P:(at + 1) * P], src, ident[:])
                        fills(ins, name + ".t", u)
                    if i >= LAG_PV + NB - 1 and (i - LAG_PV + 1) % NB < 2:
                        h, half = (i - LAG_PV + 1) // NB - 1, (i - LAG_PV + 1) % NB
                        if half == 0:
                            for v in range(NB):
                                wait_emptied(pe, name + ".t", NB * h + v)
                                if v_stage and h == 0:
                                    wait_emptied(pe, v_stage, v)
                            open_bank(name + ".o", h)
                        o = bank_of(name + ".o", h)
                        for kb in ((0, 3), (1, 2))[half]:
                            q0, q1 = a.queries(kb)
                            cols = slice(q0 * P, q1 * P)
                            at = p_place(a, h, kb, q0)
                            for m, (vp, pp) in enumerate(((0, 0), (0, 1), (1, 0))):
                                probs = pt[:, pp, at:at + q1 - q0, :].rearrange("p k q -> p (k q)")
                                ins = pe.matmul(o[:, cols], values(h, kb, vp), probs,
                                                start=(kb == 0 and m == 0), stop=(kb == 2 and m == 2),
                                                skip_group_check=True)
                        if half == 1:
                            fills(ins, name + ".o", h)

            def stacked(q, k):
                return lambda h, qs_, ks_: ((q(h)[:, qs_], k(h, 0)[:, ks_]), (q(h)[:, qs_], k(h, 1)[:, ks_]))

            def a_ready(n):
                def wait(kk):
                    pe.wait_ge(a_hi_ready, 8 * n + kk + 1)
                    pe.wait_ge(a_lo_ready, 8 * n + kk + 1)
                return wait

            def u_from(stage, n):
                def wait(kk):
                    if stage:
                        wait_emptied(pe, stage, n + kk)
                    else:
                        pe.wait_ge(u_lo_ready, n + kk + 1)
                return wait

            pe.wait_ge(ones_ready, 1)
            gemm("qi", aH, aL, True, a_ready(0), lambda: norm(1), by_rows=True)
            spread(1)
            gemm("sm", aH, aL, True)
            gemm("qb", aH, aL, False)
            pe.wait_ge(cst_landed, 32)
            pe.wait_ge(half_ready, 1)
            pe.wait_ge(split_lo, NB)
            for j in range(H):
                turn_tile("t.qi", j, lambda b: spI[:, b, j, :].bitcast(F32))
            pe.wait_ge(split_lo, NB + 2)
            for j in range(2):
                turn_tile("t.ki", j, lambda b: kdI[:, j, b, :].bitcast(F32))
            for j in range(H):
                wait_emptied(pe, "t.qi", j)
            for j in range(2):
                wait_emptied(pe, "t.ki", j)
            for i in range(24):
                h, b = i // 3, 1 + i % 3
                o = open_bank("idx", i)[:, 0:(b + 1) * P]
                for m in range(2):
                    ins = pe.matmul(o, qiS[:, h, b * P:(b + 1) * P], kiS[:, m, 0:(b + 1) * P], start=m == 0, stop=m == 1)
                fills(ins, "idx", i)
            pe.wait_ge(split_lo, NB + 4)
            for j in range(2):
                turn_tile("t.ka", j, lambda b: kdI[:, j, b, :].bitcast(F32))
            pe.wait_ge(logf_ready, 1)
            o = open_bank("cum", 0)
            for jb in range(NB):
                ins = pe.matmul(o[0:H, :], lf[:, 3, jb * H:(jb + 1) * H], tab("cum")[:, (3 - jb) * P:(3 - jb) * P + S],
                                start=(jb == 0), stop=(jb == NB - 1))
            fills(ins, "cum", 0)
            gemm("kb", aH, aL, False)
            gemm("vb", aH, aL, True)
            attention("fox", stacked(lambda h: fQ[:, h % 2, :], lambda h, m: fK[:, h % 2, m, :]),
                      lambda h, kb, m: vbS[:, m, kb, (h // 2) * P:(h // 2 + 1) * P], sp, pT, "vb")
            gemm("qa", aH, aL, True)
            gemm("ga", aH, aL, False)
            gemm("gb", aH, aL, False)
            pe.wait_ge(split_lo, 2 * NB + 6)
            for j in range(H):
                turn_tile("t.qa", j, lambda b: spA[:, b, j, :].bitcast(F32))
            for j in range(H):
                wait_emptied(pe, "t.qa", j)
            attention("dsa", stacked(lambda h: qaS[:, h, :], lambda h, m: kaS[:, m, :]),
                      lambda h, kb, m: vaS[:, m, kb, :], sp, pT)
            for n, u in enumerate(("ya0", "ya1", "yb0", "yb1")):
                gemm(u, uH, uL, False, u_from(None, 4 * (n // 2)), k_first=4 * (n // 2))
            for n in range(4):
                gemm(f"m{n}", aH, aL, False)
            for n in range(2):
                gemm(f"wo{n}", uH, uL, False, u_from(None, 8))
            pe.wait_ge(p_lo_ready, 2)
            gemm("e0", pH, pL, False, between=lambda: norm(2), by_rows=True)
            spread(2)
            gemm("e1", pH, pL, False)
            gemm("pg0", aH, aL, False, a_ready(1), by_rows=True)
            gemm("pg1", aH, aL, False)
            norm(3)
            spread(3)
            gemm("sq", aH, aL, True, a_ready(2), lambda: norm(4), by_rows=True)
            spread(4)
            gemm("skv", aH, aL, True)
            gemm("ql", aH, aL, True)
            gemm("kvl", aH, aL, True)
            pe.wait_ge(split_lo, 3 * NB + 6)
            for j in range(H):
                turn_tile("t.sq", j, lambda b: sp2[:, b, j, :].bitcast(F32))
            pe.wait_ge(split_lo, 3 * NB + 10)
            for j in range(4):
                turn_tile("t.sk", j, lambda b: kd2[:, j // 2, j % 2, b, :].bitcast(F32))
            pe.wait_ge(ql_scaled, 4)
            for j in range(3):
                turn_tile("t.cq", j, lambda b: ql[:, b, j * P:(j + 1) * P])
            pe.wait_ge(ql_scaled, 8)
            for j in range(2):
                turn_tile("t.ck", j, lambda b: kvl[:, b, j * P:(j + 1) * P])
            for j in range(H):
                wait_emptied(pe, "t.sq", j)
            for j in range(4):
                wait_emptied(pe, "t.sk", j)
            attention("swa", stacked(lambda h: sqS[:, h, :], lambda h, m: skS[:, h // 4, m, :]),
                      lambda h, kb, m: vsS[:, m, h // 4, kb, :], sc2, pT2)
            def turn_mq(i):
                pe.wait_ge(roped, 6 + 2 * NB + i)
                for j in range(4):
                    turn_tile(f"t.mq{i}", j, lambda b: uq[i][:, b, j * MQK:(j + 1) * MQK], rows=MQK)

            def turn_mk(i):
                pe.wait_ge(kr_copied, 2)
                pe.wait_ge(mk_ready, 4 * i + 4)
                for j in range(4):
                    turn_tile(f"t.mk{i}", j, lambda b: mk[i][:, b, j, :], rows=MQK)

            gemm("uq0", cqH, cqL, True, u_from("t.cq", 0))
            gemm("ukv0", ckH, ckL, True, u_from("t.ck", 0))
            turn_mq(0)
            gemm("uq1", cqH, cqL, True)
            turn_mk(0)
            gemm("ukv1", ckH, ckL, True)
            turn_mq(1)
            turn_mk(1)
            for j in range(4):
                wait_emptied(pe, "t.mk1", j)
            def mla_scores(h, qs_, ks_):
                q, k = mQ[0:MQK, h % 2], mK[0:MQK, h % 2]
                return ((q[:, 0, qs_], k[:, 0, ks_]), (q[:, 0, qs_], k[:, 1, ks_]), (q[:, 1, qs_], k[:, 0, ks_]))

            attention("mla", mla_scores,
                      lambda h, kb, m: mvS[:, m, kb, 2 * (h // 2):2 * (h // 2) + 2, :].rearrange("p h d -> p (h d)"), sc2, pT2, "ukv1")
            for n, u in enumerate(("za0", "za1", "zb0", "zb1")):
                gemm(u, uH2, uL2, False, u_from(None, 16 + 4 * (n // 2)), k_first=4 * (n // 2))
            for n in range(4):
                gemm(f"n{n}", aH, aL, False)
            for n in range(2):
                gemm(f"wp{n}", uH2, uL2, False, u_from(None, 24))
            gemm("f0", aH, aL, False, a_ready(3), lambda: norm(5), by_rows=True)
            spread(5)
            for f in range(1, DFF // 256):
                gemm(f"f{f}", aH, aL, False)
            for i in range(8):
                b, half = i // 2, i % 2
                o = open_bank("xr", i)
                for j in range(4):
                    ins = pe.transpose(o[:, j * P:(j + 1) * P], xT[:, 4 * half + j, b * P:(b + 1) * P], ident[:])
                fills(ins, "xr", i)
            first, n_chunks, _, _ = UNITS["down"]
            for c in range(first, first + n_chunks):
                pe.wait_ge(w_hi_ready, c + 1)
                pe.wait_ge(w_lo_ready, c + 1)
                wh, wl = w_view(w_hi, c), w_view(w_lo, c)
                pe.wait_ge(ff_lo, min(2 * (c - first) + 2, NF))
                per = CHUNKS[c][0]
                for i in range(8):
                    b, half = i // 2, i % 2
                    if c == first:
                        open_bank("down", i)
                    tok, col = slice(b * P, (b + 1) * P), slice(512 * half, 512 * half + 512)
                    for k in range(per):
                        kk = (c - first) * per + k
                        for m, (l, r) in enumerate(((fH, wh), (fH, wl), (fL, wh))):
                            ins = pe.matmul(bank_of("down", i)[:], l[:, kk, tok], r[:, k, col],
                                            start=(kk == 0 and m == 0), stop=(kk == NF - 1 and m == 2))
                    if c == first + n_chunks - 1:
                        fills(ins, "down", i)
                if c != first + n_chunks - 1:
                    ins.then_inc(w_used, 1)


NAMES = ["w_in", "w_branch_a", "w_branch_b", "w_merge", "w_out", "w_ple", "w_ple_gate", "b_forget",
         "w_in_2", "swa_sinks_2", "w_uq_2", "w_ukv_2", "w_o_swa_2", "w_o_mla_2", "w_out_2", "w_gate_2",
         "w_up_2", "w_down_2"]


def kernel(**inputs):
    import concourse.bacc as bacc
    from concourse.bass_utils import run_bass_kernel_spmd

    order = ["g_pre", "g_post", "g_ple", "mix_norm_g_2", "ffn_norm_g_2", "q_norm_g_2", "kv_norm_g_2"]
    arrays = {n: np.ascontiguousarray(inputs[n]) for n in NAMES}
    arrays["gains"] = np.ascontiguousarray(
        np.concatenate([np.asarray(inputs[n]).reshape(-1, P).T for n in order], axis=1))
    arrays["final_norm_g_2"] = np.ascontiguousarray(np.asarray(inputs["final_norm_g_2"]).reshape(1, D))
    arrays["xT"] = np.ascontiguousarray(np.asarray(inputs["x"])[0].T)
    arrays["pT"] = np.ascontiguousarray(np.asarray(inputs["p"])[0, 0].T)
    arrays["cst"] = constants()
    nc = bacc.Bacc("TRN2", target_bir_lowering=False, num_devices=1)
    dram = {n: nc.dram_tensor(f"in_{n}", a.shape, mybir.dt.from_np(a.dtype), kind="ExternalInput").ap()
            for n, a in arrays.items()}
    out = nc.dram_tensor("out_x", (1, S, D), F32, kind="ExternalOutput").ap()
    build(nc, dram, out)
    r = run_bass_kernel_spmd(nc, [{f"in_{n}": a for n, a in arrays.items()}], core_ids=[0])
    return r.results[0]["out_x"]
```
